# Optimizing a Trainium2 kernel written in Bass

```python
import math
import jax, jax.numpy as jnp
from jax import lax
import numpy as np
import jax
import jax.numpy as jnp

D_MODEL = 1024
BATCH = 1
SEQ = 512
DEPTH = 2

GRID_W = 64
CTX_LEN = 256
ROPE_THETA = 10000.0
NORM_EPS = 1e-6
SUBLN_EPS = 1e-5
LN_EPS = 1e-5
Q_BLOCK = 128

A_GROUPS = 8
A_WIDTH = D_MODEL // 2
A_GROUP_DIM = A_WIDTH // A_GROUPS
A_CHUNK = 128

B_HEADS = 4
B_HEAD_DIM = 64
B_V_DIM = 2 * B_HEAD_DIM
B_WIDTH = B_HEADS * B_V_DIM
B_QK = B_HEADS * 2 * B_HEAD_DIM

EVEN_IN = 3 * A_WIDTH + 2 * B_QK + 2 * B_WIDTH
EVEN_MIX = A_WIDTH + B_WIDTH
EVEN_SPLITS = (A_WIDTH, 2 * A_WIDTH, 3 * A_WIDTH, 3 * A_WIDTH + B_QK,
               3 * A_WIDTH + 2 * B_QK, 3 * A_WIDTH + 2 * B_QK + B_WIDTH)

C_HEADS = 8
C_NOPE = 128
C_ROPE = 64
C_V = 128
C_Q_RANK = 256
C_KV_RANK = 128
C_WIDTH = C_HEADS * C_V
ODD_IN = C_Q_RANK + C_KV_RANK + C_ROPE + C_WIDTH
ODD_SPLITS = (C_Q_RANK, C_Q_RANK + C_KV_RANK, C_Q_RANK + C_KV_RANK + C_ROPE)

N_EVEN = (DEPTH + 1) // 2
N_ODD = DEPTH // 2


F32 = jnp.float32

def rms_norm(x, w, eps=NORM_EPS):
    xf = x.astype(F32)
    y = xf * lax.rsqrt(jnp.mean(xf * xf, axis=-1, keepdims=True) + eps)
    return (y * w.astype(F32)).astype(x.dtype)

def layer_norm(x, w, b, eps=LN_EPS):
    xf = x.astype(F32)
    mu = jnp.mean(xf, axis=-1, keepdims=True)
    xc = xf - mu
    y = xc * lax.rsqrt(jnp.mean(xc * xc, axis=-1, keepdims=True) + eps)
    return (y * w.astype(F32) + b.astype(F32)).astype(x.dtype)

def adaln_terms(cond, w_ada, b_ada):
    m = jax.nn.silu(cond) @ w_ada + b_ada
    return jnp.split(m, 3, axis=-1)

def axial_rope_tables(seq, dim):
    rows = seq // GRID_W
    row = jnp.repeat(jnp.arange(rows), GRID_W).astype(F32)
    col = jnp.tile(jnp.arange(GRID_W), rows).astype(F32)
    half = dim // 2
    inv = ROPE_THETA ** (-jnp.arange(0, half, 2, dtype=F32) / half)
    ang_r = row[:, None] * inv[None, :]
    ang_c = col[:, None] * inv[None, :]
    ang = jnp.concatenate([ang_r, ang_r, ang_c, ang_c], axis=-1)
    return jnp.cos(ang), jnp.sin(ang)

def apply_rope(x, cos, sin):
    extra = x.ndim - 3
    shp = (1, cos.shape[0]) + (1,) * extra + (cos.shape[1],)
    c = cos.reshape(shp)
    s = sin.reshape(shp)
    seg = x.reshape(x.shape[:-1] + (2, 2, x.shape[-1] // 4))
    rot = jnp.concatenate([-seg[..., 1:, :], seg[..., :1, :]], axis=-2).reshape(x.shape)
    return (x.astype(F32) * c + rot.astype(F32) * s).astype(x.dtype)

def sweep_query_blocks(fn, q):
    b, s = q.shape[0], q.shape[1]
    nb = s // Q_BLOCK
    qb = jnp.moveaxis(q.reshape((b, nb, Q_BLOCK) + q.shape[2:]), 1, 0)
    ob = lax.map(fn, qb)
    return jnp.moveaxis(ob, 0, 1).reshape((b, s) + ob.shape[3:])

def spatial_gating(u, v, w_s, b_s, ln_w, ln_b):
    bsz, length, _ = v.shape
    vn = layer_norm(v, ln_w, ln_b)
    vc = vn.reshape(bsz, length // A_CHUNK, A_CHUNK, A_GROUPS, A_GROUP_DIM)
    mixed = jnp.einsum('gpq,bnqgd->bnpgd', w_s, vc) + b_s.T[None, None, :, :, None]
    return u * mixed.reshape(bsz, length, A_WIDTH)

def diff_attn_core(q, k, v, lam):
    s = jnp.einsum('bqhmd,bkhmd->bhmqk', q, k).astype(F32) * (B_HEAD_DIM ** -0.5)
    p = jax.nn.softmax(s, axis=-1)
    a = p[:, :, 0] - lam * p[:, :, 1]
    return jnp.einsum('bhqk,bkhd->bqhd', a.astype(v.dtype), v)

def mla_core(q, k, v):
    s = jnp.einsum('bqhd,bkhd->bhqk', q, k).astype(F32) * ((C_NOPE + C_ROPE) ** -0.5)
    p = jax.nn.softmax(s, axis=-1)
    return jnp.einsum('bhqk,bkhd->bqhd', p.astype(v.dtype), v)

def even_mixer(xl, xc, need_ctx, li, w_in, w_s, b_s, ln_w, ln_b, lq1, lk1, lq2, lk2, subln_w, w_out):
    bsz, seq, _ = xl.shape
    clen = xc.shape[1]
    cos, sin = axial_rope_tables(seq, B_HEAD_DIM)
    lam_init = 0.8 - 0.6 * math.exp(-0.3 * li)
    lam = (jnp.exp(jnp.sum(lq1.astype(F32) * lk1.astype(F32)))
           - jnp.exp(jnp.sum(lq2.astype(F32) * lk2.astype(F32))) + lam_init)

    au_l, av_l, az_l, bq_l, bk_l, bv_l, bz_l = jnp.split(xl @ w_in, EVEN_SPLITS, axis=-1)
    au_c, av_c, az_c, bq_c, bk_c, bv_c, bz_c = jnp.split(xc @ w_in, EVEN_SPLITS, axis=-1)

    def a_branch(u, v, z):
        return spatial_gating(jax.nn.gelu(u, approximate=False), jax.nn.gelu(v, approximate=False),
                              w_s, b_s, ln_w, ln_b) * jax.nn.silu(z)

    def b_post(o, z, length):
        o = rms_norm(o, subln_w, SUBLN_EPS) * (1.0 - lam_init)
        return o.reshape(bsz, length, B_WIDTH) * jax.nn.silu(z)

    qk_shape_l = (bsz, seq, B_HEADS, 2, B_HEAD_DIM)
    qk_shape_c = (bsz, clen, B_HEADS, 2, B_HEAD_DIM)
    q_l = apply_rope(bq_l.reshape(qk_shape_l), cos, sin)
    k_l = apply_rope(bk_l.reshape(qk_shape_l), cos, sin)
    v_l = bv_l.reshape(bsz, seq, B_HEADS, B_V_DIM)
    k_c = bk_c.reshape(qk_shape_c)
    v_c = bv_c.reshape(bsz, clen, B_HEADS, B_V_DIM)
    k_all = jnp.concatenate([k_c, k_l], axis=1)
    v_all = jnp.concatenate([v_c, v_l], axis=1)

    ob_l = sweep_query_blocks(lambda qb: diff_attn_core(qb, k_all, v_all, lam), q_l)
    out_l = jnp.concatenate([a_branch(au_l, av_l, az_l), b_post(ob_l, bz_l, seq)], axis=-1) @ w_out

    out_c = None
    if need_ctx:
        q_c = bq_c.reshape(qk_shape_c)
        ob_c = diff_attn_core(q_c, k_c, v_c, lam)
        out_c = jnp.concatenate([a_branch(au_c, av_c, az_c), b_post(ob_c, bz_c, clen)], axis=-1) @ w_out
    return out_l, out_c

def odd_mixer(xl, xc, need_ctx, w_in, q_norm_w, wq_b, kv_norm_w, wkv_b, w_out):
    bsz, seq, _ = xl.shape
    clen = xc.shape[1]
    cos, sin = axial_rope_tables(seq, C_ROPE)

    cq_l, ckv_l, kr_l, z_l = jnp.split(xl @ w_in, ODD_SPLITS, axis=-1)
    cq_c, ckv_c, kr_c, z_c = jnp.split(xc @ w_in, ODD_SPLITS, axis=-1)

    def queries(cq, length):
        q = (rms_norm(cq, q_norm_w) @ wq_b).reshape(bsz, length, C_HEADS, C_NOPE + C_ROPE)
        return q[..., :C_NOPE], q[..., C_NOPE:]

    def keys_values(ckv, k_rope, length):
        kv = (rms_norm(ckv, kv_norm_w) @ wkv_b).reshape(bsz, length, C_HEADS, C_NOPE + C_V)
        k_rope_h = jnp.broadcast_to(k_rope[:, :, None, :], (bsz, length, C_HEADS, C_ROPE))
        return jnp.concatenate([kv[..., :C_NOPE], k_rope_h], axis=-1), kv[..., C_NOPE:]

    qn_l, qr_l = queries(cq_l, seq)
    q_l = jnp.concatenate([qn_l, apply_rope(qr_l, cos, sin)], axis=-1)
    kr_l_rot = apply_rope(kr_l[:, :, None, :], cos, sin)[:, :, 0, :]
    k_l, v_l = keys_values(ckv_l, kr_l_rot, seq)
    k_c, v_c = keys_values(ckv_c, kr_c, clen)
    k_all = jnp.concatenate([k_c, k_l], axis=1)
    v_all = jnp.concatenate([v_c, v_l], axis=1)

    o_l = sweep_query_blocks(lambda qb: mla_core(qb, k_all, v_all), q_l)
    out_l = (o_l.reshape(bsz, seq, C_WIDTH) * jax.nn.silu(z_l)) @ w_out

    out_c = None
    if need_ctx:
        qn_c, qr_c = queries(cq_c, clen)
        q_c = jnp.concatenate([qn_c, qr_c], axis=-1)
        o_c = mla_core(q_c, k_c, v_c)
        out_c = (o_c.reshape(bsz, clen, C_WIDTH) * jax.nn.silu(z_c)) @ w_out
    return out_l, out_c

def first_inputs(seed: int = 0) -> dict:
    key = jax.random.key(seed)
    ks = jax.random.split(key, 32)
    nrm = jax.random.normal
    D = D_MODEL
    return {
        'x': nrm(ks[0], (BATCH, SEQ, D), F32),
        'c': nrm(ks[1], (BATCH, D), F32),
        'ctx': nrm(ks[2], (BATCH, CTX_LEN, D), F32),
        'c_ctx': nrm(ks[3], (D,), F32),
        'norm_w': 1.0 + 0.02 * nrm(ks[4], (DEPTH, D), F32),
        'ada_w': 0.5 * D ** -0.5 * nrm(ks[5], (DEPTH, D, 3 * D), F32),
        'ada_b': 0.01 * nrm(ks[6], (DEPTH, 3 * D), F32),
        'even_w_in': D ** -0.5 * nrm(ks[7], (N_EVEN, D, EVEN_IN), F32),
        'a_ws': A_CHUNK ** -0.5 * nrm(ks[8], (N_EVEN, A_GROUPS, A_CHUNK, A_CHUNK), F32),
        'a_bs': 1.0 + 0.02 * nrm(ks[9], (N_EVEN, A_GROUPS, A_CHUNK), F32),
        'a_ln_w': 1.0 + 0.02 * nrm(ks[10], (N_EVEN, A_WIDTH), F32),
        'a_ln_b': 0.01 * nrm(ks[11], (N_EVEN, A_WIDTH), F32),
        'b_lq1': 0.1 * nrm(ks[12], (N_EVEN, B_HEAD_DIM), F32),
        'b_lk1': 0.1 * nrm(ks[13], (N_EVEN, B_HEAD_DIM), F32),
        'b_lq2': 0.1 * nrm(ks[14], (N_EVEN, B_HEAD_DIM), F32),
        'b_lk2': 0.1 * nrm(ks[15], (N_EVEN, B_HEAD_DIM), F32),
        'b_subln_w': 1.0 + 0.02 * nrm(ks[16], (N_EVEN, B_V_DIM), F32),
        'even_w_out': EVEN_MIX ** -0.5 * nrm(ks[17], (N_EVEN, EVEN_MIX, D), F32),
        'odd_w_in': D ** -0.5 * nrm(ks[18], (N_ODD, D, ODD_IN), F32),
        'c_q_norm_w': 1.0 + 0.02 * nrm(ks[19], (N_ODD, C_Q_RANK), F32),
        'c_wq_b': C_Q_RANK ** -0.5 * nrm(ks[20], (N_ODD, C_Q_RANK, C_HEADS * (C_NOPE + C_ROPE)), F32),
        'c_kv_norm_w': 1.0 + 0.02 * nrm(ks[21], (N_ODD, C_KV_RANK), F32),
        'c_wkv_b': C_KV_RANK ** -0.5 * nrm(ks[22], (N_ODD, C_KV_RANK, C_HEADS * (C_NOPE + C_V)), F32),
        'odd_w_out': C_WIDTH ** -0.5 * nrm(ks[23], (N_ODD, C_WIDTH, D), F32),
        'final_w': 1.0 + 0.02 * nrm(ks[24], (D,), F32),
    }

def first_block(x, c, ctx, c_ctx, norm_w, ada_w, ada_b, even_w_in, a_ws, a_bs, a_ln_w, a_ln_b,
              b_lq1, b_lk1, b_lq2, b_lk2, b_subln_w, even_w_out, odd_w_in, c_q_norm_w, c_wq_b,
              c_kv_norm_w, c_wkv_b, odd_w_out, final_w):
    h_lat, h_ctx = x, ctx
    for li in range(DEPTH):
        need_ctx = li < DEPTH - 1
        shift_l, scale_l, gate_l = adaln_terms(c, ada_w[li], ada_b[li])
        shift_c, scale_c, gate_c = adaln_terms(c_ctx, ada_w[li], ada_b[li])
        xl = rms_norm(h_lat, norm_w[li]) * (1.0 + scale_l[:, None, :]) + shift_l[:, None, :]
        xc = rms_norm(h_ctx, norm_w[li]) * (1.0 + scale_c) + shift_c
        if li % 2 == 0:
            e = li // 2
            out_l, out_c = even_mixer(xl, xc, need_ctx, li, even_w_in[e], a_ws[e], a_bs[e],
                                      a_ln_w[e], a_ln_b[e], b_lq1[e], b_lk1[e], b_lq2[e], b_lk2[e],
                                      b_subln_w[e], even_w_out[e])
        else:
            o = li // 2
            out_l, out_c = odd_mixer(xl, xc, need_ctx, odd_w_in[o], c_q_norm_w[o], c_wq_b[o],
                                     c_kv_norm_w[o], c_wkv_b[o], odd_w_out[o])
        h_lat = h_lat + gate_l[:, None, :] * out_l
        if need_ctx:
            h_ctx = h_ctx + gate_c * out_c
    return rms_norm(h_lat, final_w)


DEPTH_2 = 1

HEAD_DIM = 64
ATTN_HEADS = 8
ATTN_KV_HEADS = 2
GQA_GROUP = ATTN_HEADS // ATTN_KV_HEADS
RET_HEADS = 4
RET_QK_DIM = 64
RET_V_DIM = 128
ATTN_WIDTH = ATTN_HEADS * HEAD_DIM
RET_WIDTH = RET_HEADS * RET_V_DIM
MIX_WIDTH = ATTN_WIDTH + RET_WIDTH
PROJ_SIZES = (ATTN_WIDTH, ATTN_KV_HEADS * HEAD_DIM, ATTN_KV_HEADS * HEAD_DIM,
              RET_HEADS * RET_QK_DIM, RET_HEADS * RET_QK_DIM, RET_WIDTH, RET_WIDTH)
PROJ_DIM = sum(PROJ_SIZES)
PROJ_SPLITS = tuple(int(v) for v in np.cumsum(PROJ_SIZES)[:-1])
RET_CHUNK = 128
ROPE_AXIS_DIM = HEAD_DIM // 2
N_GROUPS = 4
EXPERTS_PER_GROUP = 8
N_EXPERTS = N_GROUPS * EXPERTS_PER_GROUP
TOP_K_IN_GROUP = 2
D_EXPERT = 512
MOE_BLOCK = 128
EPS = 1e-6


def _rmsnorm(x, g):
    xf = x.astype(jnp.float32)
    xf = xf * lax.rsqrt(jnp.mean(xf * xf, axis=-1, keepdims=True) + EPS)
    return xf.astype(x.dtype) * g

def _modulate(xn, shift, scale):
    return xn * (1.0 + scale) + shift

def _axial_rope_tables(rows):
    row = jnp.repeat(jnp.arange(rows), GRID_W).astype(jnp.float32)
    col = jnp.tile(jnp.arange(GRID_W), rows).astype(jnp.float32)
    freqs = ROPE_THETA ** (-jnp.arange(0, ROPE_AXIS_DIM, 2, dtype=jnp.float32) / ROPE_AXIS_DIM)
    ang = jnp.concatenate([row[:, None] * freqs, col[:, None] * freqs], axis=-1)
    return jnp.cos(ang), jnp.sin(ang)

def _rope(x, cos, sin):
    B, L, H, d = x.shape
    xp = x.astype(jnp.float32).reshape(B, L, H, d // 2, 2)
    x0, x1 = xp[..., 0], xp[..., 1]
    c = cos[None, :, None, :]
    s = sin[None, :, None, :]
    out = jnp.stack([x0 * c - x1 * s, x0 * s + x1 * c], axis=-1).reshape(B, L, H, d)
    return out.astype(x.dtype)

def _attend(q, k, v):
    B, L, _, _ = q.shape
    nb = L // Q_BLOCK
    qb = jnp.moveaxis(q.reshape(B, nb, Q_BLOCK, ATTN_KV_HEADS, GQA_GROUP, HEAD_DIM), 1, 0)
    scale = HEAD_DIM ** -0.5

    def one_block(q_blk):
        s = jnp.einsum('bqhgd,bkhd->bhgqk', q_blk, k).astype(jnp.float32) * scale
        p = jax.nn.softmax(s, axis=-1)
        return jnp.einsum('bhgqk,bkhd->bqhgd', p.astype(v.dtype), v)

    o = lax.map(one_block, qb)
    return jnp.moveaxis(o, 0, 1).reshape(B, L, ATTN_WIDTH)

def _head_rms(x, g):
    xf = x.astype(jnp.float32)
    xf = xf * lax.rsqrt(jnp.mean(xf * xf, axis=-1, keepdims=True) + EPS)
    return xf.astype(x.dtype) * g

def _ret_heads(q, k, v, cos, sin):
    B, L, _ = q.shape
    q = q.reshape(B, L, RET_HEADS, RET_QK_DIM)
    k = k.reshape(B, L, RET_HEADS, RET_QK_DIM)
    if cos is not None:
        q = _rope(q, cos, sin)
        k = _rope(k, cos, sin)
    q = jnp.transpose(q, (0, 2, 1, 3)).astype(jnp.float32)
    k = jnp.transpose(k, (0, 2, 1, 3)).astype(jnp.float32) * (RET_QK_DIM ** -0.5)
    v = jnp.transpose(v.reshape(B, L, RET_HEADS, RET_V_DIM), (0, 2, 1, 3)).astype(jnp.float32)
    return q, k, v

def _retention_state(k, v, log_g, reverse):
    Lc = k.shape[2]
    m = jnp.arange(Lc, dtype=jnp.float32)
    dist = m if reverse else (Lc - 1 - m)
    w = jnp.exp(log_g[:, None] * dist[None, :])
    return jnp.einsum('bhmk,bhmv,hm->bhkv', k, v, w)

def _retention_chunked(q, k, v, log_g, s0, include_diag):
    B, H, L, dk = q.shape
    dv = v.shape[-1]
    C = RET_CHUNK
    n = L // C
    qc = q.reshape(B, H, n, C, dk)
    kc = k.reshape(B, H, n, C, dk)
    vc = v.reshape(B, H, n, C, dv)
    pos = jnp.arange(C, dtype=jnp.float32)
    diff = pos[:, None] - pos[None, :]
    mask = (diff >= 0) if include_diag else (diff > 0)
    dmat = jnp.where(mask, jnp.exp(log_g[:, None, None] * jnp.where(mask, diff, 0.0)[None]), 0.0)
    scores = jnp.einsum('bhnik,bhnjk->bhnij', qc, kc) * dmat[None, :, None]
    intra = jnp.einsum('bhnij,bhnjv->bhniv', scores, vc)
    zeta = jnp.exp(log_g[:, None] * (C - 1 - pos)[None, :])
    u = jnp.einsum('bhnjk,bhnjv,hj->bhnkv', kc, vc, zeta)
    g_chunk = jnp.exp(log_g * C)[None, :, None, None]

    def step(s, u_n):
        return g_chunk * s + u_n, s

    s_final, s_prev = lax.scan(step, s0, jnp.moveaxis(u, 2, 0))
    xi = jnp.exp(log_g[:, None] * (pos + 1.0)[None, :])
    cross = jnp.einsum('bhnik,nbhkv,hi->bhniv', qc, s_prev, xi)
    return (intra + cross).reshape(B, H, L, dv), s_final

def _retention_latent(q, k, v, k_c, v_c, log_gf, log_gb):
    s_f = _retention_state(k_c, v_c, log_gf, reverse=False)
    s_b = _retention_state(k_c, v_c, log_gb, reverse=True)
    o_f, _ = _retention_chunked(q, k, v, log_gf, s_f, True)
    o_b, _ = _retention_chunked(jnp.flip(q, 2), jnp.flip(k, 2), jnp.flip(v, 2), log_gb, s_b, False)
    return o_f + jnp.flip(o_b, 2)

def _retention_context(q, k, v, log_gf, log_gb):
    B, H, _, dk = q.shape
    s0 = jnp.zeros((B, H, dk, v.shape[-1]), jnp.float32)
    o_f, _ = _retention_chunked(q, k, v, log_gf, s0, True)
    o_b, _ = _retention_chunked(jnp.flip(q, 2), jnp.flip(k, 2), jnp.flip(v, 2), log_gb, s0, False)
    return o_f + jnp.flip(o_b, 2)

def _ret_output(o, gn_g, gn_b, gate, dtype):
    B, H, L, dv = o.shape
    mu = jnp.mean(o, axis=-1, keepdims=True)
    var = jnp.mean(jnp.square(o - mu), axis=-1, keepdims=True)
    on = (o - mu) * lax.rsqrt(var + EPS)
    on = jnp.transpose(on, (0, 2, 1, 3)).reshape(B, L, H * dv).astype(dtype)
    return (on * gn_g + gn_b) * jax.nn.silu(gate)

def _hier_moe(h, w_grp, b_grp, w_exp, b_exp, w_gate, w_up, w_down):
    T, D = h.shape
    grp_p = jax.nn.softmax((h @ w_grp).astype(jnp.float32) + b_grp, axis=-1)
    p_g, g_idx = lax.top_k(grp_p, 1)
    exp_logits = ((h @ w_exp).astype(jnp.float32) + b_exp).reshape(T, N_GROUPS, EXPERTS_PER_GROUP)
    sel = jnp.take_along_axis(exp_logits, jnp.broadcast_to(g_idx[:, :, None], (T, 1, EXPERTS_PER_GROUP)), axis=1)[:, 0]
    p_e, j_idx = lax.top_k(jax.nn.softmax(sel, axis=-1), TOP_K_IN_GROUP)
    weights = p_g * (p_e / jnp.sum(p_e, axis=-1, keepdims=True))
    eid = (g_idx * EXPERTS_PER_GROUP + j_idx).astype(jnp.int32)

    A = T * TOP_K_IN_GROUP
    eid_f = eid.reshape(A)
    tok_f = jnp.repeat(jnp.arange(T, dtype=jnp.int32), TOP_K_IN_GROUP)
    w_f = weights.reshape(A)
    order = jnp.argsort(eid_f)
    e_s, tok_s, w_s = eid_f[order], tok_f[order], w_f[order]
    counts = jnp.zeros((N_EXPERTS,), jnp.int32).at[eid_f].add(1)
    starts = jnp.cumsum(counts) - counts
    pcounts = (counts + MOE_BLOCK - 1) // MOE_BLOCK * MOE_BLOCK
    pends = jnp.cumsum(pcounts)
    pstarts = pends - pcounts
    dest = pstarts[e_s] + (jnp.arange(A, dtype=jnp.int32) - starts[e_s])
    P = A + N_EXPERTS * MOE_BLOCK
    nblk = P // MOE_BLOCK
    buf_tok = jnp.full((P,), T, jnp.int32).at[dest].set(tok_s)
    buf_w = jnp.zeros((P,), jnp.float32).at[dest].set(w_s).astype(h.dtype)
    blk_start = jnp.arange(nblk, dtype=jnp.int32) * MOE_BLOCK
    blk_e = jnp.minimum(jnp.sum(blk_start[:, None] >= pends[None, :], axis=1), N_EXPERTS - 1)
    h_pad = jnp.concatenate([h, jnp.zeros((1, D), h.dtype)], axis=0)
    xb = h_pad[buf_tok].reshape(nblk, MOE_BLOCK, D)

    def expert_block(args):
        x_blk, e = args
        return (jax.nn.silu(x_blk @ w_gate[e]) * (x_blk @ w_up[e])) @ w_down[e]

    yb = lax.map(expert_block, (xb, blk_e)).reshape(P, D)
    out = jnp.zeros((T + 1, D), h.dtype).at[buf_tok].add(yb * buf_w[:, None])
    return out[:T]

def second_inputs(seed: int = 0) -> dict:
    key = jax.random.key(seed)
    ks = jax.random.split(key, 32)
    f32 = jnp.float32

    def nrm(k, shape, scale):
        return jax.random.normal(k, shape, f32) * scale

    base_logit = jnp.asarray(np.log(2.0 ** (5 + np.arange(RET_HEADS)) - 1.0).astype(np.float32))
    return {
        "x": nrm(ks[0], (BATCH, SEQ, D_MODEL), 1.0),
        "c": nrm(ks[1], (BATCH, D_MODEL), 1.0),
        "ctx": nrm(ks[2], (BATCH, CTX_LEN, D_MODEL), 1.0),
        "c_ctx": nrm(ks[3], (D_MODEL,), 1.0),
        "w_ada": nrm(ks[4], (DEPTH_2, D_MODEL, 6 * D_MODEL), 0.5 * D_MODEL ** -0.5),
        "b_ada": nrm(ks[5], (DEPTH_2, 6 * D_MODEL), 0.01),
        "norm1_g": 1.0 + nrm(ks[6], (DEPTH_2, D_MODEL), 0.05),
        "w_in": nrm(ks[7], (DEPTH_2, D_MODEL, PROJ_DIM), D_MODEL ** -0.5),
        "attn_q_norm": 1.0 + nrm(ks[8], (DEPTH_2, HEAD_DIM), 0.05),
        "attn_k_norm": 1.0 + nrm(ks[9], (DEPTH_2, HEAD_DIM), 0.05),
        "ret_decay_fwd": base_logit + nrm(ks[10], (DEPTH_2, RET_HEADS), 0.1),
        "ret_decay_bwd": base_logit + nrm(ks[11], (DEPTH_2, RET_HEADS), 0.1),
        "ret_gn_g": 1.0 + nrm(ks[12], (DEPTH_2, RET_WIDTH), 0.05),
        "ret_gn_b": nrm(ks[13], (DEPTH_2, RET_WIDTH), 0.01),
        "w_out": nrm(ks[14], (DEPTH_2, MIX_WIDTH, D_MODEL), MIX_WIDTH ** -0.5),
        "norm2_g": 1.0 + nrm(ks[15], (DEPTH_2, D_MODEL), 0.05),
        "moe_w_grp": nrm(ks[16], (DEPTH_2, D_MODEL, N_GROUPS), D_MODEL ** -0.5),
        "moe_b_grp": nrm(ks[17], (DEPTH_2, N_GROUPS), 0.01),
        "moe_w_exp": nrm(ks[18], (DEPTH_2, D_MODEL, N_EXPERTS), D_MODEL ** -0.5),
        "moe_b_exp": nrm(ks[19], (DEPTH_2, N_EXPERTS), 0.01),
        "moe_w_gate": nrm(ks[20], (DEPTH_2, N_EXPERTS, D_MODEL, D_EXPERT), D_MODEL ** -0.5),
        "moe_w_up": nrm(ks[21], (DEPTH_2, N_EXPERTS, D_MODEL, D_EXPERT), D_MODEL ** -0.5),
        "moe_w_down": nrm(ks[22], (DEPTH_2, N_EXPERTS, D_EXPERT, D_MODEL), D_EXPERT ** -0.5),
        "final_norm_g": 1.0 + nrm(ks[23], (D_MODEL,), 0.05),
    }

def second_block(x, c, ctx, c_ctx, w_ada, b_ada, norm1_g, w_in, attn_q_norm, attn_k_norm,
              ret_decay_fwd, ret_decay_bwd, ret_gn_g, ret_gn_b, w_out, norm2_g,
              moe_w_grp, moe_b_grp, moe_w_exp, moe_b_exp, moe_w_gate, moe_w_up, moe_w_down,
              final_norm_g):
    B, L, D = x.shape
    CL = ctx.shape[1]
    ROWS = L // GRID_W
    cos, sin = _axial_rope_tables(ROWS)

    for l in range(DEPTH_2):
        mod_x = (jax.nn.silu(c) @ w_ada[l] + b_ada[l])[:, None, :]
        mod_c = (jax.nn.silu(c_ctx) @ w_ada[l] + b_ada[l])[None, None, :]
        sh1, sc1, gt1, sh2, sc2, gt2 = jnp.split(mod_x, 6, axis=-1)
        csh1, csc1, cgt1, csh2, csc2, cgt2 = jnp.split(mod_c, 6, axis=-1)
        log_gf = jax.nn.log_sigmoid(ret_decay_fwd[l].astype(jnp.float32))
        log_gb = jax.nn.log_sigmoid(ret_decay_bwd[l].astype(jnp.float32))

        hx = _modulate(_rmsnorm(x, norm1_g[l]), sh1, sc1)
        hc = _modulate(_rmsnorm(ctx, norm1_g[l]), csh1, csc1)
        qa, ka, va, qr, kr, vr, gr = jnp.split(hx @ w_in[l], PROJ_SPLITS, axis=-1)
        qa_c, ka_c, va_c, qr_c, kr_c, vr_c, gr_c = jnp.split(hc @ w_in[l], PROJ_SPLITS, axis=-1)

        qa = _rope(_head_rms(qa.reshape(B, L, ATTN_HEADS, HEAD_DIM), attn_q_norm[l]), cos, sin)
        ka = _rope(_head_rms(ka.reshape(B, L, ATTN_KV_HEADS, HEAD_DIM), attn_k_norm[l]), cos, sin)
        va = va.reshape(B, L, ATTN_KV_HEADS, HEAD_DIM)
        ka_c = _head_rms(ka_c.reshape(B, CL, ATTN_KV_HEADS, HEAD_DIM), attn_k_norm[l])
        va_c = va_c.reshape(B, CL, ATTN_KV_HEADS, HEAD_DIM)
        attn_x = _attend(qa, jnp.concatenate([ka_c, ka], axis=1), jnp.concatenate([va_c, va], axis=1))

        q_r, k_r, v_r = _ret_heads(qr, kr, vr, cos, sin)
        q_rc, k_rc, v_rc = _ret_heads(qr_c, kr_c, vr_c, None, None)
        ret_o = _retention_latent(q_r, k_r, v_r, k_rc, v_rc, log_gf, log_gb)
        ret_x = _ret_output(ret_o, ret_gn_g[l], ret_gn_b[l], gr, x.dtype)

        x_new = x + gt1 * (jnp.concatenate([attn_x, ret_x], axis=-1) @ w_out[l])

        h2 = _modulate(_rmsnorm(x_new, norm2_g[l]), sh2, sc2)
        y = _hier_moe(h2.reshape(B * L, D), moe_w_grp[l], moe_b_grp[l], moe_w_exp[l], moe_b_exp[l],
                      moe_w_gate[l], moe_w_up[l], moe_w_down[l]).reshape(B, L, D)
        x_new = x_new + gt2 * y

        if l + 1 < DEPTH_2:
            qa_c = _head_rms(qa_c.reshape(B, CL, ATTN_HEADS, HEAD_DIM), attn_q_norm[l])
            attn_c = _attend(qa_c, ka_c, va_c)
            ret_c = _ret_output(_retention_context(q_rc, k_rc, v_rc, log_gf, log_gb),
                                ret_gn_g[l], ret_gn_b[l], gr_c, ctx.dtype)
            ctx_new = ctx + cgt1 * (jnp.concatenate([attn_c, ret_c], axis=-1) @ w_out[l])
            h2c = _modulate(_rmsnorm(ctx_new, norm2_g[l]), csh2, csc2)
            yc = _hier_moe(h2c.reshape(B * CL, D), moe_w_grp[l], moe_b_grp[l], moe_w_exp[l], moe_b_exp[l],
                           moe_w_gate[l], moe_w_up[l], moe_w_down[l]).reshape(B, CL, D)
            ctx = ctx_new + cgt2 * yc
        x = x_new

    return _rmsnorm(x, final_norm_g)


def setup_inputs(seed=0):
    out = dict(first_inputs(seed))
    for name, value in second_inputs(seed + 1).items():
        if name != "x":
            out[name + "_2"] = value
    return out


def reference(
    x, c, ctx, c_ctx, norm_w, ada_w, ada_b, even_w_in, a_ws, a_bs, a_ln_w, a_ln_b, b_lq1, b_lk1,
    b_lq2, b_lk2, b_subln_w, even_w_out, odd_w_in, c_q_norm_w, c_wq_b, c_kv_norm_w, c_wkv_b,
    odd_w_out, final_w, c_2, ctx_2, c_ctx_2, w_ada_2, b_ada_2, norm1_g_2, w_in_2, attn_q_norm_2,
    attn_k_norm_2, ret_decay_fwd_2, ret_decay_bwd_2, ret_gn_g_2, ret_gn_b_2, w_out_2, norm2_g_2,
    moe_w_grp_2, moe_b_grp_2, moe_w_exp_2, moe_b_exp_2, moe_w_gate_2, moe_w_up_2, moe_w_down_2,
    final_norm_g_2,
):
    x = first_block(
        x, c, ctx, c_ctx, norm_w, ada_w, ada_b, even_w_in, a_ws, a_bs, a_ln_w, a_ln_b, b_lq1,
        b_lk1, b_lq2, b_lk2, b_subln_w, even_w_out, odd_w_in, c_q_norm_w, c_wq_b, c_kv_norm_w,
        c_wkv_b, odd_w_out, final_w,
    )
    return second_block(
        x, c_2, ctx_2, c_ctx_2, w_ada_2, b_ada_2, norm1_g_2, w_in_2, attn_q_norm_2,
        attn_k_norm_2, ret_decay_fwd_2, ret_decay_bwd_2, ret_gn_g_2, ret_gn_b_2, w_out_2,
        norm2_g_2, moe_w_grp_2, moe_b_grp_2, moe_w_exp_2, moe_b_exp_2, moe_w_gate_2, moe_w_up_2,
        moe_w_down_2, final_norm_g_2,
    )


_drawn_inputs = setup_inputs


def setup_inputs(seed=0):
    import zlib

    import numpy as np

    out = dict(_drawn_inputs(seed))
    spreads = {}
    factors = {'norm_w': 7.422,
     'ada_b': 4.306,
     'a_bs': 8.0,
     'a_ln_w': 8.0,
     'a_ln_b': 8.0,
     'b_lq1': 7.433,
     'b_lk1': 3.922,
     'b_lq2': 64.0,
     'b_lk2': 7.066,
     'b_subln_w': 8.0,
     'c_q_norm_w': 8.0,
     'c_wq_b': 2.695,
     'c_kv_norm_w': 8.0,
     'b_ada_2': 4.392,
     'norm1_g_2': 3.706,
     'attn_q_norm_2': 8.0,
     'attn_k_norm_2': 8.0,
     'ret_gn_g_2': 5.265,
     'ret_gn_b_2': 8.0,
     'norm2_g_2': 2.753,
     'moe_b_grp_2': 6.347,
     'moe_b_exp_2': 8.0}
    for name, (base, spread) in spreads.items():
        noise = np.random.default_rng([zlib.crc32(name.encode()), seed]).standard_normal(out[name].shape)
        drawn = base * np.exp(spread * noise) if base else spread * noise
        out[name] = jnp.asarray(drawn.astype(out[name].dtype))
    for name, factor in factors.items():
        out[name] = (out[name] * factor).astype(out[name].dtype)
    return out
```

```python
from contextlib import ExitStack

import numpy as np
import concourse.bass as bass
from concourse import mybir

ALU = mybir.AluOpType
ACT = mybir.ActivationFunctionType
F32 = mybir.dt.float32
F32R = mybir.dt.float32r
AX = mybir.AxisListType.X

P = 128
D = 1024
KT = D // P
CTX, SEQ = 256, 512
TOK = CTX + SEQ
CT, LT = CTX // P, SEQ // P
NT = CT + LT
EPS, SUBLN_EPS, LN_EPS = 1e-6, 1e-5, 1e-5
LAM_INIT = 0.8 - 0.6 * 1.0
PIECE = 2048
RAW, SPLIT = 3, 4
SLOTS = 4
E_HEADS, E_SCALE = 4, 64 ** -0.5
O_HEADS, O_SCALE = 8, 192 ** -0.5
S_HEADS, S_SCALE = 8, 64 ** -0.5
S_UNITS = LT * S_HEADS
R_HEADS = 4
R_TABLE = 1152
S_RUN = {"odd": 16, "gqa": S_UNITS}
E_UNITS = NT * E_HEADS
KB = 1024
GROUPS, EXPERTS, WIDTH = 4, 32, 512
SLOTS_E = 2 * SEQ
BLOCKS = SLOTS_E // P + EXPERTS - 1
PARTS = 6
FAR = 1e30

VEC = {}
_at = 0
for _name, _n in (("norm0", 8), ("norm1", 8), ("norm2", 8), ("ada0", 24), ("ada1", 24), ("ada2", 48),
                  ("spatial_b", 8), ("q_norm", 2), ("kv_norm", 1), ("decay", 8)):
    VEC[_name] = slice(_at, _at + _n)
    _at += _n
VECS = _at


def with_context(layer, c):
    return layer == 0 or c < 4


class Plan:

    def __init__(self):
        self.jobs, self.pieces = {}, []

    def job(self, *name):
        assert name not in self.jobs, name
        self.jobs[name] = len(self.jobs)
        return name

    def piece(self, name, source, kind):
        self.pieces.append(dict(name=name, source=source, kind=kind, last=None))

    def finish(self):
        self.number = {p["name"]: g for g, p in enumerate(self.pieces)}
        self.splits = [p for p in self.pieces if p["kind"] == "split"]
        self.through = {}
        for k, p in enumerate(self.splits):
            p["k"] = k
            self.through[p["name"][0:2]] = k + 1
        writers = [j for j in self.jobs if j[0] in ("norm", "mix")]
        self.xt = {j: n for n, j in enumerate(writers)}


def make_plan(src):
    plan = Plan()
    late = []

    def ada(layer, chunks):
        for c in chunks:
            late.append((layer, c, plan.job("ada", layer, c)))

    def stream_late():
        for layer, c, job in late:
            for h in range(2):
                plan.piece(("ada", layer, c, h), src[f"ada{layer}"][c, h], "raw")
                plan.pieces[-1]["last"] = job
        late.clear()

    def chunk(layer, what, c, jobs):
        for h in range(2):
            plan.piece((layer, what, h), src[layer][c, h], "split")
        for j in jobs:
            job = plan.job(layer, what, j)
        for p in plan.pieces[-2:]:
            p["last"] = job
        stream_late()

    tiles = range(NT)
    for c in range(4):
        plan.job("ada", 0, c)
    for kt in range(KT):
        plan.job("norm", "even", kt)
    chunk("even", "av", 1, tiles)
    ada(0, [4])
    chunk("even", "au", 0, tiles)
    ada(0, [5])
    chunk("even", "az", 2, tiles)
    ada(1, [0])
    chunk("even", "bv", 5, tiles)
    for g in range(8):
        plan.job("spatial", g)
    ada(1, [1])
    chunk("even", "bz", 6, tiles)
    for s in range(2):
        plan.job("gate", 0, s)
    ada(1, [2])
    chunk("even", "bq", 3, range(4))
    for f in range(4):
        plan.job("rope", "q", f)
    ada(1, [3])
    chunk("even", "bk", 4, range(4))
    for f in range(4):
        plan.job("rope", "k", f)
    for kt in range(4):
        plan.job("mix", "a", kt)
    for u in range(2):
        plan.job("S", "even", u, 0)
        plan.job("S", "even", u, 1)
    for u in range(E_UNITS):
        plan.job("T", "even", u)
        if u + 2 < E_UNITS:
            plan.job("S", "even", u + 2, 0)
            plan.job("S", "even", u + 2, 1)
        plan.job("O", "even", u)
    for kt in range(4, 8):
        plan.job("mix", "b", kt)
    chunk("eout", "o", 0, tiles)
    ada(1, [4])
    chunk("eout", "p", 1, tiles)
    ada(1, [5])

    lat = range(CT, NT)
    for kt in range(KT):
        plan.job("norm", "odd", kt)
    chunk("odd", "a", 0, tiles)
    ada(2, [0])
    chunk("odd", "z", 1, lat)
    for kt in range(2):
        plan.job("turn", "cq", kt)
    plan.job("turn", "ckv", 0)
    plan.job("turn", "kr", 0)
    plan.job("rope", "kr", 0)
    ada(2, [1])
    chunk("odd", "y", 2, lat)
    ada(2, [2])
    for g in range(2):
        for what, n in (("q", 6), ("kv", 4)):
            plan.piece((what, g), src[what][g], "split")
            if what == "q":
                stream_late()
            for f in range(n):
                job = plan.job(what, g, f)
            if what == "kv":
                for m in tiles:
                    job = plan.job("v", g, m)
            plan.pieces[-1]["last"] = job
            for p in plan.pieces:
                if p["name"] == (what, g):
                    p["last"] = job
        for j in range(2):
            plan.job("rope", "qr", 2 * g + j)
        for u in range(2):
            plan.job("S", "odd", 16 * g + u)
        for u in range(16):
            plan.job("T", "odd", 16 * g + u)
            if u + 2 < 16:
                plan.job("S", "odd", 16 * g + u + 2)
            plan.job("O", "odd", 16 * g + u)
        ada(2, [3 + g])
    plan.job("gate", 1, 0)
    for kt in range(KT):
        plan.job("mix", "odd", kt)
    chunk("oout", "o", 0, lat)
    ada(2, [5])
    chunk("oout", "p", 1, lat)
    ada(2, [6])

    for kt in range(KT):
        plan.job("norm", "second", kt)
    chunk("second", "qa", 0, lat)
    ada(2, [7])
    chunk("second", "kk", 1, tiles)
    ada(2, [8])
    chunk("second", "vr", 2, tiles)
    ada(2, [9])
    chunk("second", "gr", 3, lat)
    ada(2, [10])
    chunk("second", "qr", 4, lat)
    for kt in range(4):
        plan.job("turn", "qa", kt)
    plan.job("turn", "ka", 0)
    for kt in range(2):
        plan.job("turn", "qr2", kt)
        plan.job("turn", "kr2", kt)
    ada(2, [11])
    plan.job("gate", 2, 0)
    for u in range(2):
        plan.job("S", "gqa", u)
    for u in range(S_UNITS):
        plan.job("T", "gqa", u)
        if u + 2 < S_UNITS:
            plan.job("S", "gqa", u + 2)
        plan.job("O", "gqa", u)
    for a in range(NT):
        plan.job("R", 0, a)
    for h in range(R_HEADS):
        for a in range(NT):
            if a == 2:
                plan.job("RO", h)
            if h + 1 < R_HEADS:
                plan.job("R", h + 1, a)
    for kt in range(KT):
        plan.job("mix", "second", kt)
    chunk("sout", "o", 0, lat)
    chunk("sout", "p", 1, lat)
    stream_late()

    plan.job("free", 0)
    plan.job("gate", 2, 1)
    plan.job("gate", 2, 2)
    for kt in range(KT):
        plan.job("turn", "h2", kt)
    plan.job("router")
    plan.job("free", 1)
    plan.job("counts")
    plan.job("starts")
    plan.job("gate", 2, 3)
    plan.finish()
    return plan


def build(nc, src, out):
    plan = make_plan(src)
    jobs, pieces, splits, number = plan.jobs, plan.pieces, plan.splits, plan.number
    z_dram = nc.dram_tensor("z_dram", [NT, P, 512], F32).ap()
    h_dram = nc.dram_tensor("h_dram", [LT, P, D], F32).ap()
    y_dram = nc.dram_tensor("y_dram", [LT, P, D], F32).ap()
    x2_dram = nc.dram_tensor("x2_dram", [LT, P, D], F32).ap()
    pair_dram = nc.dram_tensor("pair_dram", [(BLOCKS + 1) * P, D], F32).ap()

    with ExitStack() as stack:
        def sb(name, shape, dt=F32):
            return stack.enter_context(nc.sbuf_tensor(name, shape, dt))

        def sem(name):
            return stack.enter_context(nc.semaphore(name))

        raw = sb("raw", [P, RAW, PIECE])
        split_base = (nc.sbuf_base + 31) // 32 * 32
        whi = sb("whi", [P, SPLIT, PIECE], F32R)
        wlo = sb("wlo", [P, SPLIT, PIECE], F32R)
        xt_base = (nc.sbuf_base + 31) // 32 * 32
        sb("xt_region", [P, 12 * KB])
        g_base = (nc.sbuf_base + 31) // 32 * 32
        sb("g_region", [P, 12 * KB])

        def at(name, base, offset, shape, dt=F32):
            return nc.alloc_sbuf_tensor_at(name, shape, dt, offset=base + offset)

        early = at("early", split_base, 0, [P, 8, PIECE])
        xth = at("xth", xt_base, 0, [P, KT, TOK], F32R)
        xtl = at("xtl", xt_base, 24 * KB, [P, KT, TOK], F32R)
        p0 = at("p0", xt_base, 12 * KB, [P, 3, TOK])
        z_in = at("z_in", xt_base, 21 * KB, [P, 512])
        p1 = at("p1", xt_base, 36 * KB, [P, 2, TOK])
        pt = at("pt", xt_base, 42 * KB, [P, 2, TOK])
        ao = at("ao", g_base, 0, [P, NT, 512])
        o_rows = at("o_rows", g_base, 0, [P, NT, 512])
        vv = at("vv", g_base, 12 * KB, [P, NT, 512])
        qt = at("qt", g_base, 12 * KB, [P, 4, TOK])
        kt_ = at("kt_", g_base, 24 * KB, [P, 4, TOK])
        vb = at("vb", g_base, 36 * KB, [P, NT, 512])
        h_rows = at("h_rows", g_base, 12 * KB, [P, NT, D])
        a_rows = at("a_rows", g_base, 0, [P, NT, 512])
        cqh = at("cqh", g_base, 12 * KB, [P, 2, SEQ], F32R)
        cql = at("cql", g_base, 16 * KB, [P, 2, SEQ], F32R)
        ckvh = at("ckvh", g_base, 20 * KB, [P, TOK], F32R)
        ckvl = at("ckvl", g_base, 23 * KB, [P, TOK], F32R)
        kr_t = at("kr_t", g_base, 26 * KB, [P, TOK])
        cq_f = at("cq_f", g_base, 29 * KB, [P, 2, SEQ])
        ckv_f = at("ckv_f", g_base, 33 * KB, [P, TOK])
        oo_rows = at("oo_rows", g_base, 29 * KB, [P, LT, D])
        ptb = [at("pt0", g_base, 45 * KB, [P, TOK]), at("pt1", g_base, 0, [P, TOK])]
        y_in = at("y_in", g_base, 3 * KB, [P, 2, D])
        k_n = at("k_n", xt_base, 0, [P, 4, TOK])
        v_o = at("v_o", xt_base, 12 * KB, [P, NT, 512])
        q_n = at("q_n", xt_base, 24 * KB, [P, 4, SEQ])
        q_r = at("q_r", xt_base, 32 * KB, [P, 2, SEQ])
        po = at("po", xt_base, 36 * KB, [P, 3, TOK])
        qa = at("qa", g_base, 0, [P, LT, 512])
        kk = at("kk", g_base, 8 * KB, [P, NT, 512])
        vr = at("vr", g_base, 20 * KB, [P, NT, 512])
        gr = at("gr", g_base, 32 * KB, [P, LT, 512])
        qr = at("qr", g_base, 40 * KB, [P, LT, 256])
        qa_t = at("qa_t", xt_base, 0, [P, 4, SEQ])
        ka_t = at("ka_t", xt_base, 8 * KB, [P, TOK])
        qr_t = at("qr_t", xt_base, 11 * KB, [P, 2, SEQ])
        kr2_t = at("kr2_t", xt_base, 15 * KB, [P, 2, TOK])
        pg = at("pg", xt_base, 21 * KB, [P, 3, TOK])
        ptg = at("ptg", xt_base, 30 * KB, [P, 2, TOK])
        sw = at("sw", xt_base, 21 * KB, [P, NT, SEQ])
        dist = at("dist", xt_base, 36 * KB, [P, R_TABLE])
        w_lat = at("w_lat", xt_base, 41 * KB, [P, 896])
        w_ctx = at("w_ctx", xt_base, 44 * KB + 512, [P, 640])
        oa_rows = at("oa_rows", g_base, 0, [P, LT, 512])
        or_rows = at("or_rows", g_base, 40 * KB, [P, LT, 512])

        h2 = at("h2", g_base, 0, [P, LT, D])
        h2h = at("h2h", xt_base, 0, [P, LT, D], F32R)
        h2l = at("h2l", xt_base, 16 * KB, [P, LT, D], F32R)
        h2_t = at("h2_t", xt_base, 32 * KB, [P, KT, SEQ])
        xe_rows = at("xe_rows", g_base, 16 * KB, [P, D])
        xeh = at("xeh", xt_base, 32 * KB, [P, KT, P], F32R)
        xel = at("xel", xt_base, 36 * KB, [P, KT, P], F32R)
        hot = at("hot", xt_base, 40 * KB, [P, LT, P], F32R)
        hid = at("hid", xt_base, 42 * KB, [P, WIDTH])
        hth = at("hth", xt_base, 44 * KB, [P, 4, P], F32R)
        htl = at("htl", xt_base, 46 * KB, [P, 4, P], F32R)
        pairs = at("pairs", xt_base, 0, [P, LT, 2, D])
        gt2 = at("gt2", g_base, 0, [P, D])
        final_g = at("final_g", g_base, 4 * KB, [P, D])

        ident = sb("ident", [P, P])
        rope_perm = sb("rope_perm", [P, P])
        cos_t = sb("cos_t", [P, SEQ])
        sin_t = sb("sin_t", [P, SEQ])
        vecs = sb("vecs", [P, VECS])
        cvec = sb("cvec", [P, 2, KT, 2])
        mod = [sb("mod0", [P, 24, 2]), sb("mod1", [P, 24, 2]), sb("mod2", [P, 48, 2])]
        scale_t = sb("scale_t", [P, KT, 2])
        tmp = sb("tmp", [P, 2, TOK])
        stat = sb("stat", [P, 192])
        half = sb("half", [P, 2])
        gate_base = (nc.sbuf_base + 31) // 32 * 32
        sb("gate_region", [P, 2 * KB])
        gate_rows = at("gate_rows", gate_base, 0, [P, 2, D])
        spatial_w = at("spatial_w", gate_base, 0, [P, 8, P])
        ln_w = at("ln_w", gate_base, 4 * KB, [P, 512])
        ln_b = at("ln_b", gate_base, 6 * KB, [P, 512])
        misc_base = (nc.sbuf_base + 31) // 32 * 32
        sb("misc_region", [P, 512])
        lamv = at("lamv", misc_base, 0, [P, 4, 64])
        acc = at("acc", misc_base, 0, [P, 512])
        junk = tmp[:, 1, 512:768].bitcast(mybir.dt.bfloat16)
        final_w = at("final_w", gate_base, 4 * KB, [P, D])
        gn = at("gn", gate_base, 4 * KB, [P, 2, 512])
        subln = sb("subln", [P, P])
        weh = [whi[:, i, :] for i in range(SPLIT)] + [
            at("weh4", g_base, 0, [P, PIECE], F32R)[:], at("weh5", g_base, 36 * KB, [P, PIECE], F32R)[:]]
        wel = [wlo[:, i, :] for i in range(SPLIT)] + [
            at("wel4", g_base, 8 * KB, [P, PIECE], F32R)[:], at("wel5", gate_base, 0, [P, PIECE], F32R)[:]]
        y_rows = tmp[:].rearrange("p a b -> p (a b)")[:, 0:D]
        route = subln[:, 72:104]
        rc = cos_t
        col = rc[:, 0:P]
        before = rc[:, P:2 * P]
        ones = rc[:, 2 * P:3 * P]
        block_first = rc[:, 384:384 + BLOCKS + 1]
        thresholds = rc[:, 424:428]
        falling = rc[:, 428:460]
        router_w = sin_t[:, 0:KT * 36].rearrange("p (k n) -> p k n", k=KT)
        router_b = sin_t[:, 288:324]
        where = sin_t[:, 324:324 + 4 * (BLOCKS + 1)]
        blocks_i = subln[:, 0:48].bitcast(mybir.dt.int32)
        dest = subln[:, 48:56]
        dest_i = subln[:, 56:64].bitcast(mybir.dt.uint32)
        pair_w = subln[:, 64:72]
        ps = stack.enter_context(nc.psum_tensor("ps", [P, 2 * SLOTS, 512], F32))

        ss = stat[:, 0:6]
        rstd = stat[:, 6:12]
        lam2 = stat[:, 12:14]
        nlam = stat[:, 14:15]
        bn = stat[:, 16:52]
        mv = stat[:, 52:64]
        oss = stat[:, 64:88]
        orstd = stat[:, 88:112]
        soft = stat[:, 112:176].rearrange("p (r c) -> p r c", c=8)
        ss2 = stat[:, 64:76].rearrange("p (h m) -> p h m", h=2)
        osum = stat[:, 12:60]
        rstats = stat[:, 12:64]
        lg = stat[:, 180:188]
        lgt = stat[:, 188:192]

        s_raw = [sem(f"s_raw{i}") for i in range(RAW)]
        s_hi, s_lo = sem("s_hi"), sem("s_lo")
        s_mm = [sem(f"s_mm{i}") for i in range(SLOTS)]
        s_ev = [sem(f"s_ev{i}") for i in range(SLOTS)]
        s_act, s_dve, s_pool = sem("s_act"), sem("s_dve"), sem("s_pool")
        s_const, s_const2, s_c, s_cvec = sem("s_const"), sem("s_const2"), sem("s_c"), sem("s_cvec")
        s_x = [sem(f"s_x_{m}") for m in range(NT)]
        s_early = [sem(f"s_early{c}") for c in range(4)]
        s_acc, s_acc0 = sem("s_acc"), sem("s_acc0")
        s_ss, s_rstd, s_xn, s_half = sem("s_ss"), sem("s_rstd"), sem("s_xn"), sem("s_half")
        s_xhi, s_xlo = sem("s_xhi"), sem("s_xlo")
        s_lam0, s_lam1 = sem("s_lam0"), sem("s_lam1")
        s_ag, s_lnr, s_vn = sem("s_ag"), sem("s_lnr"), sem("s_vn")
        s_z = [sem(f"s_z{i}") for i in range(2)]
        s_zin, s_q, s_k, s_nb, s_comb = sem("s_zin"), sem("s_q"), sem("s_k"), sem("s_nb"), sem("s_comb")
        s_oss, s_ors, s_post = sem("s_oss"), sem("s_ors"), sem("s_post")
        s_xr, s_h, s_spill = sem("s_xr"), sem("s_h"), sem("s_spill")
        s_sq, s_rs2, s_xn2 = sem("s_sq"), sem("s_rs2"), sem("s_xn2")
        s_ao, s_cp, s_cn = sem("s_ao"), sem("s_cp"), sem("s_cn")
        s_y = [sem(f"s_y{i}") for i in range(2)]
        s_yin = [sem(f"s_yin{i}") for i in range(2)]
        s_kr, s_qr, s_ct_hi, s_ct_lo = sem("s_kr"), sem("s_qr"), sem("s_ct_hi"), sem("s_ct_lo")
        s_nbo, s_oy = sem("s_nbo"), sem("s_oy")
        s_hr, s_h2, s_fw, s_first, s_x2st = sem("s_hr"), sem("s_h2"), sem("s_fw"), sem("s_first"), sem("s_x2st")
        s_ctx2, s_rt, s_sn, s_sp, s_qn = sem("s_ctx2"), sem("s_rt"), sem("s_sn"), sem("s_sp"), sem("s_qn")
        s_nbg, s_dist, s_lg, s_lge = sem("s_nbg"), sem("s_dist"), sem("s_lg"), sem("s_lge")
        s_arg, s_wl, s_wc, s_gs, s_gp, s_ret = sem("s_arg"), sem("s_wl"), sem("s_wc"), sem("s_gs"), sem("s_gp"), sem("s_ret")
        s_gnl, s_h3r, s_h3 = sem("s_gnl"), sem("s_h3r"), sem("s_h3")
        s_out = sem("s_out")

        s_mods, s_row2, s_h2h, s_h2l = sem("s_mods"), sem("s_row2"), sem("s_h2h"), sem("s_h2l")
        s_rcl, s_gd, s_ge, s_rw, s_chosen, s_blocks = (sem(n) for n in (
            "s_rcl", "s_gd", "s_ge", "s_rw", "s_chosen", "s_blocks"))
        s_nblk, s_fill = sem("s_nblk"), sem("s_fill")
        s_ew = [sem(f"s_ew{i}") for i in range(RAW)]
        s_eh = sem("s_eh")
        s_el = sem("s_el")
        s_used = sem("s_used")
        s_hot, s_gat, s_rows, s_turned, s_xeh, s_xel = (sem(n) for n in (
            "s_hot", "s_gat", "s_rows", "s_turned", "s_xeh", "s_xel"))
        s_silu, s_hid, s_tr, s_hth, s_htl = (sem(n) for n in ("s_silu", "s_hid", "s_tr", "s_hth", "s_htl"))
        s_yev, s_yst = sem("s_yev"), sem("s_yst")
        s_fgl, s_pair, s_x4, s_fin = sem("s_fgl"), [sem(f"s_pair{m}") for m in range(LT)], sem("s_x4"), sem("s_fin")

        def slot(job):
            n = jobs[job] % SLOTS
            return ps[:, 2 * n:2 * n + 2, :].rearrange("p b n -> p (b n)")

        def slot_at(n):
            return ps[:, 2 * n:2 * n + 2, :].rearrange("p b n -> p (b n)")

        def filled(eng, *job):
            n = jobs[job]
            eng.wait_ge(s_mm[n % SLOTS], n // SLOTS + 1)
            return slot(job)

        def evacuated(eng, *job):
            n = jobs[job]
            eng.wait_ge(s_ev[n % SLOTS], n // SLOTS + 1)

        def ev(*job):
            return s_ev[jobs[job] % SLOTS], jobs[job] // SLOTS + 1

        def landed(eng, g):
            eng.wait_ge(s_raw[g % RAW], 16 * (g // RAW + 1))

        class Own:

            def __init__(self, eng, s):
                self.eng, self.s, self.count = eng, s, {}

            def free(self, ins, s=None):
                s = s or self.s
                if isinstance(s, tuple):
                    self.last = s
                else:
                    n = self.count[s.name] = self.count.get(s.name, 0) + 1
                    self.last = s, n
                ins.then_inc(self.last[0], 1)

            def wait(self):
                self.eng.wait_ge(*self.last)

            def __call__(self, ins, s=None):
                self.free(ins, s)
                self.wait()

        def keys(m):
            return CTX if m < CT else TOK

        block = stack.enter_context(nc.Block())

        @block.sync
        def _(sp):
            sp.dma_start(cvec[:], src["cvec"]).then_inc(s_c, 16)
            sp.dma_start(vecs[:], src["vecs"]).then_inc(s_const, 16)
            sp.dma_start(ident[:], src["ident"]).then_inc(s_const, 16)
            for c in range(4):
                for h in range(2):
                    sp.dma_start(early[:, 2 * c + h, :], src["ada0"][c, h]).then_inc(s_early[c], 16)
            for g, p in enumerate(pieces):
                if g >= RAW:
                    old = pieces[g - RAW]
                    if old["kind"] == "split":
                        sp.wait_ge(s_hi, old["k"] + 1)
                        sp.wait_ge(s_lo, old["k"] + 1)
                    else:
                        filled(sp, *old["last"])
                width = p["source"].shape[-1]
                sp.dma_start(raw[:, g % RAW, 0:width], p["source"]).then_inc(s_raw[g % RAW], 16)
            for i in range(PARTS):
                sp.wait_ge(s_el, i + 1)
                sp.dma_start(raw[:, i % RAW, :], src["experts"][0, i]).then_inc(s_ew[i % RAW], 16)
            sp.wait_ge(s_blocks, 1)
            blocks = sp.value_load(blocks_i[0:1, 41:42], min_val=8, max_val=BLOCKS)
            with sp.Fori(1, blocks) as j:
                e = sp.value_load(blocks_i[0:1, bass.ds(j, 1)], min_val=0, max_val=EXPERTS - 1)
                for i in range(PARTS):
                    sp.wait_ge(s_el, PARTS * j + i + 1)
                    sp.dma_start(raw[:, i % RAW, :], src["experts"][bass.ds(e, 1), i].rearrange("a p n -> (a p) n"))\
                        .then_inc(s_ew[i % RAW], 16)
            for m in range(LT):
                sp.wait_ge(s_fin, m + 1)
                sp.dma_start(out[P * m:P * m + P, :], h_rows[:, CT + m, :]).then_inc(s_out, 16)
            sp.wait_ge(s_out, 16 * LT)

        @block.gpsimd
        def _(pool):
            own = Own(pool, s_pool)
            for m in list(range(CT, NT)) + list(range(CT)):
                pool.dma_start(h_rows[:, m, :], src["x"][m]).then_inc(s_x[m], 16)
            nc.gpsimd.memset(half[:, 0:1], -0.5).then_inc(s_half, 1)
            nc.gpsimd.memset(half[:, 1:2], 1.0).then_inc(s_half, 1)
            for dst, name in ((rope_perm, "rope_perm"), (cos_t, "cos_t"), (sin_t, "sin_t"), (spatial_w, "spatial_w"),
                              (ln_w, "ln_w"), (ln_b, "ln_b"), (lamv, "lamv"), (subln, "subln")):
                pool.dma_start(dst[:], src[name]).then_inc(s_const2, 16)

            def powers(dst, source, n, eps, ready):
                own(nc.gpsimd.tensor_scalar(dst, source, 1.0 / n, eps, ALU.mult, ALU.add))
                own.wait()
                nc.gpsimd.tensor_tensor(dst, dst, half[:, 0:1].broadcast_to([P, dst.shape[1]]), ALU.pow).then_inc(ready, 1)

            pool.wait_ge(s_half, 2)
            pool.wait_ge(s_ss, NT)
            powers(rstd, ss, D, EPS, s_rstd)
            pool.wait_ge(s_ag, NT)
            powers(mv.rearrange("p (m c) -> p m c", c=2)[:, :, 1], mv.rearrange("p (m c) -> p m c", c=2)[:, :, 1],
                   1, LN_EPS, s_lnr)
            for m in range(NT):
                evacuated(pool, "even", "bz", m)
                pool.dma_start(z_dram[m], tmp[:, m % 2, 0:512]).then_inc(s_z[m % 2], 16)
            for i in range(2):
                pool.wait_ge(s_z[i], 16 * 3)
            filled(pool, "mix", "a", 3)
            for m in range(NT):
                if m:
                    pool.wait_ge(s_post, m)
                pool.dma_start(z_in[:], z_dram[m]).then_inc(s_zin, 16)
                pool.wait_ge(s_oss, m + 1)
                powers(orstd[:, 4 * m:4 * m + 4], oss[:, 4 * m:4 * m + 4], P, SUBLN_EPS, s_ors)
            filled(pool, "S", "even", E_UNITS - 1, 1)
            for m in range(NT):
                pool.dma_start(h_rows[:, m, :], src["x"][m]).then_inc(s_xr, 16)

            def row_powers(n, ready):
                pool.wait_ge(s_sq, n)
                own(nc.gpsimd.tensor_tensor(ss, ss2[:, 0, :], ss2[:, 1, :], ALU.add))
                powers(rstd, ss, D, EPS, ready)

            for m in range(LT):
                pool.wait_ge(s_h, NT + CT + m + 1)
                pool.dma_start(h_dram[m], h_rows[:, CT + m, :]).then_inc(s_spill, 16)
            row_powers(2 * NT, s_rs2)
            pool.wait_ge(s_ao, NT)
            powers(osum[:, 12:18], osum[:, 0:6], 256, EPS, s_cp)
            powers(osum[:, 18:24], osum[:, 6:12], P, EPS, s_cp)
            for c, what in enumerate("zy"):
                for m in range(CT, NT):
                    evacuated(pool, "odd", what, m)
                    pool.dma_start(y_dram[m - CT][:, 512 * c:512 * c + 512], tmp[:, m % 2, 0:512])\
                        .then_inc(s_y[m % 2], 16)
            for i in range(2):
                pool.wait_ge(s_y[i], 16 * 4)
            filled(pool, "turn", "ckv", 0)
            filled(pool, "turn", "kr", 0)
            for m in range(2):
                pool.dma_start(y_in[:, m, :], y_dram[m]).then_inc(s_yin[m], 16)
            for m in range(2, LT):
                pool.wait_ge(s_oy, m - 1)
                pool.dma_start(y_in[:, m % 2, :], y_dram[m]).then_inc(s_yin[m % 2], 16)
            pool.dma_start(final_w[:], src["final_w"]).then_inc(s_fw, 16)
            filled(pool, "mix", "odd", KT - 1)
            pool.wait_ge(s_spill, 16 * LT)
            for m in range(LT):
                pool.dma_start(h_rows[:, CT + m, :], h_dram[m]).then_inc(s_hr, 16)
            for m in range(CT):
                pool.dma_start(h_rows[:, m, :], src["ctx2"][m]).then_inc(s_ctx2, 16)
            row_powers(2 * NT + 2 * LT, s_rs2)
            pool.wait_ge(s_first, LT)
            for m in range(LT):
                pool.dma_start(x2_dram[m], h_rows[:, CT + m, :]).then_inc(s_x2st, 16)
            pool.dma_start(gn[:], src["gn"]).then_inc(s_gnl, 16)
            for dst, name in ((cos_t, "cos_r"), (sin_t, "sin_r"), (subln, "qk_norm")):
                pool.dma_start(dst[:, 0:src[name].shape[-1]], src[name]).then_inc(s_rt, 16)
            row_powers(2 * NT + 2 * LT + 2 * NT, s_rs2)
            pool.wait_ge(s_sn, NT + LT)
            powers(osum[:, 0:44], osum[:, 0:44], 64, EPS, s_sp)
            evacuated(pool, "second", "qr", NT - 1)
            nc.gpsimd.iota(dist[:], [[1, R_TABLE]], base=-384, channel_multiplier=-1,
                           allow_small_or_imprecise_dtypes=True).then_inc(s_dist, 1)
            for h in range(R_HEADS):
                pool.wait_ge(s_gs, LT * (h + 1))
                v = rstats[:, 8 * h:8 * h + 8].rearrange("p (m c) -> p m c", c=2)[:, :, 1]
                powers(v, v, 1, EPS, s_gp)
            filled(pool, "mix", "second", KT - 1)
            pool.wait_ge(s_x2st, 16 * LT)
            for m in range(LT):
                pool.dma_start(h_rows[:, CT + m, :], x2_dram[m]).then_inc(s_h3r, 16)

            pool.dma_start(rc[:], src["route_c"]).then_inc(s_rcl, 16)
            pool.dma_start(sin_t[:, 0:324], src["router"]).then_inc(s_rcl, 16)
            pool.dma_start(vecs[:, VEC["norm2"]], src["norm2_g"]).then_inc(s_rcl, 16)
            row_powers(2 * NT + 2 * LT + 2 * NT + 2 * LT, s_rs2)
            pool.wait_ge(s_blocks, 1)
            last = pool.value_load(blocks_i[0:1, 40:41], min_val=7, max_val=BLOCKS - 1)

            blocks = pool.value_load(blocks_i[0:1, 41:42], min_val=8, max_val=BLOCKS)
            unused = pool.value_load(blocks_i[0:1, 42:43], min_val=1, max_val=BLOCKS - 7)
            with pool.Fori(blocks, BLOCKS + 1) as j:
                pool.dma_start(pair_dram[bass.ds(j * P, P), :], h_rows[:, CT, :]).then_inc(s_fill, 16)

            pool.dma_start(x2_dram[0], h_rows[:, CT, :]).then_inc(s_yst, 16)

            def store(j):
                pool.wait_ge(s_yev, j + 2)
                pool.dma_start(pair_dram[bass.ds(j * P, P), :], y_rows).then_inc(s_yst, 16)

            with pool.Fori(0, last) as j:
                store(j)
            store(last)
            pool.dma_start(final_g[:], src["final_g"]).then_inc(s_fgl, 16)
            pool.wait_ge(s_yst, 16 * last + 32)
            pool.wait_ge(s_fill, 16 * unused)
            own(nc.gpsimd.tensor_tensor(route[:, 30:31], half[:, 0:1], half[:, 0:1], ALU.mult))
            for m in range(LT):
                for c in range(2):
                    nc.gpsimd.indirect_dma_start(
                        pairs[:, m, c, :], None, pair_dram,
                        bass.IndirectOffsetOnAxis(ap=dest_i[:, 4 * c + m:4 * c + m + 1], axis=0)).then_inc(s_pair[m], 16)
            row_powers(2 * NT + 2 * LT + 2 * NT + 4 * LT, s_rs2)

        @block.scalar
        def _(act):
            own = Own(act, s_act)
            made = [0]

            def split_high(upto):
                upto = upto if isinstance(upto, int) else plan.through[upto]
                while made[0] < min(upto, len(splits)):
                    k = made[0]
                    w = splits[k]["source"].shape[-1]
                    landed(act, number[splits[k]["name"]])
                    if k >= SPLIT:
                        filled(act, *splits[k - SPLIT]["last"])
                    own(nc.scalar.activation(whi[:, k % SPLIT, 0:w], raw[:, number[splits[k]["name"]] % RAW, 0:w],
                                         ACT.Copy), s_hi)
                    made[0] += 1

            act.wait_ge(s_c, 16)
            own(nc.scalar.activation(cvec[:], cvec[:], ACT.Silu), s_cvec)
            for m in list(range(CT, NT)) + list(range(CT)):
                act.wait_ge(s_x[m], 16)
                spare = ao[:, 0:2, :].rearrange("p a b -> p (a b)")
                own(nc.scalar.activation(spare, h_rows[:, m, :], ACT.Square, accum_out=ss[:, m:m + 1]), s_ss)
                act.wait_ge(s_ss, (m - CT) % NT + 1)
            act.wait_ge(s_rstd, 1)
            for m in range(NT):
                own.free(nc.scalar.activation(h_rows[:, m, :], h_rows[:, m, :], ACT.Copy, scale=rstd[:, m:m + 1]), s_xn)
            filled(act, "ada", 0, 3)
            split_high(2)
            for kt in range(KT):
                evacuated(act, "norm", "even", kt)
                own(nc.scalar.activation(xth[:, kt, :], tmp[:, kt % 2, :], ACT.Copy), s_xhi)
            split_high(4)

            def chunk(c, layer, what, func, dst):
                split_high(2 * (c + 2))
                for m in range(NT):
                    v = filled(act, layer, what, m)
                    own(nc.scalar.activation(dst(m), v[:, 0:512], func), ev(layer, what, m))

            chunk(0, "even", "av", ACT.Gelu, lambda m: vv[:, m, :])
            chunk(1, "even", "au", ACT.Gelu, lambda m: ao[:, m, :])
            split_high(2 * (2 + 2))
            for m in range(NT):
                v = filled(act, "even", "az", m)
                if m >= 2:
                    act.wait_ge(s_vn, m - 1)
                own(nc.scalar.activation(tmp[:, m % 2, 0:512], v[:, 0:512], ACT.Silu), ev("even", "az", m))
            act.wait_ge(s_lam0, 1)
            own(nc.scalar.activation(lam2, lam2, ACT.Exp), s_lam1)
            chunk(3, "even", "bv", ACT.Copy, lambda m: vb[:, m, :])
            split_high(2 * (4 + 2))
            act.wait_ge(s_vn, NT)
            for m in range(NT):
                v = filled(act, "even", "bz", m)
                if m >= 2:
                    act.wait_ge(s_z[m % 2], 16 * (m // 2))
                own(nc.scalar.activation(tmp[:, m % 2, 0:512], v[:, 0:512], ACT.Silu), ev("even", "bz", m))
            for s in range(2):
                v = filled(act, "gate", 0, s)
                own(nc.scalar.activation(gate_rows[:, s, :], v, ACT.Copy), ev("gate", 0, s))
            for c, what, dst in ((5, "bq", qt), (6, "bk", kt_)):
                split_high(2 * (c + 2))
                for f in range(4):
                    v = filled(act, "even", what, f)
                    own(nc.scalar.activation(dst[:, f, CTX:TOK], v[:, 0:SEQ], ACT.Copy))
                    own(nc.scalar.activation(dst[:, f, 0:CTX], v[:, SEQ:TOK], ACT.Copy), ev("even", what, f))
            for kt in range(4):
                v = filled(act, "mix", "a", kt)
                own(nc.scalar.activation(xth[:, kt, :], v[:, 0:TOK], ACT.Copy), s_xhi)

            def exps(u):
                m = u // 4
                for i, pbuf in ((0, p0[:, u % 3, 0:keys(m)]), (1, p1[:, u % 2, 0:keys(m)])):
                    if i == 0 and u >= 3:
                        filled(act, "T", "even", u - 3)
                    if i == 1 and u >= 2:
                        act.wait_ge(s_comb, u - 1)
                    act.wait_ge(s_nb, 2 * u + i + 1)
                    st = soft[:, u % 4, :]
                    own(nc.scalar.activation(pbuf, slot(("S", "even", u, i))[:, 0:keys(m)], ACT.Exp,
                                         bias=st[:, 2 + i:3 + i], scale=E_SCALE,
                                         accum_out=st[:, 4 + i:5 + i]), ev("S", "even", u, i))

            exps(0)
            exps(1)
            for u in range(E_UNITS):
                v = filled(act, "T", "even", u)
                if u >= 2:
                    filled(act, "O", "even", u - 2)
                n = keys(u // 4)
                own(nc.scalar.activation(pt[:, u % 2, 0:n], v[:, 0:n], ACT.Copy), ev("T", "even", u))
                if u + 2 < E_UNITS:
                    exps(u + 2)
            for kt in range(4, 8):
                v = filled(act, "mix", "b", kt)
                own(nc.scalar.activation(xth[:, kt, :], v[:, 0:TOK], ACT.Copy), s_xhi)
            for what, nxt in (("o", ("eout", "p")), ("p", ("odd", "a"))):
                split_high(nxt)

            squared = [0]

            def squares(tiles, ready, count):
                for m in tiles:
                    act.wait_ge(ready, count(m))
                    for h in range(2):
                        own(nc.scalar.activation(junk, h_rows[:, m, 512 * h:512 * h + 512], ACT.Square,
                                                 accum_out=ss2[:, h, m:m + 1]), s_sq)

            def norm_high(stage):
                for kt in range(KT):
                    evacuated(act, "norm", stage, kt)
                    own(nc.scalar.activation(xth[:, kt, :], tmp[:, kt % 2, :], ACT.Copy), s_xhi)

            squares(range(NT), s_h, lambda m: NT + m + 1)
            split_high(("odd", "a"))
            norm_high("odd")
            split_high(("odd", "z"))
            for m in range(NT):
                v = filled(act, "odd", "a", m)
                own(nc.scalar.activation(a_rows[:, m, :], v[:, 0:512], ACT.Copy), ev("odd", "a", m))
            for c, (what, nxt) in enumerate((("z", ("odd", "y")), ("y", ("q", 0)))):
                split_high(nxt)
                if c == 1:
                    for kt in range(2):
                        evacuated(act, "turn", "cq", kt)
                        own(nc.scalar.activation(cqh[:, kt, :], cq_f[:, kt, :], ACT.Copy), s_ct_hi)
                    evacuated(act, "turn", "ckv", 0)
                    own(nc.scalar.activation(ckvh[:], ckv_f[:], ACT.Copy), s_ct_hi)
                    v = filled(act, "turn", "kr", 0)
                    own(nc.scalar.activation(kr_t[:], v[:, 0:TOK], ACT.Copy), ev("turn", "kr", 0))
                act.wait_ge(s_ao, NT)
                for m in range(CT, NT):
                    v = filled(act, "odd", what, m)
                    n = 2 * c + (m - CT) // 2
                    if n:
                        act.wait_ge(s_y[m % 2], 16 * n)
                    own(nc.scalar.activation(tmp[:, m % 2, 0:512], v[:, 0:512], ACT.Silu), ev("odd", what, m))

            def exps(stage, u, pbuf, nb, scale):
                if u % S_RUN[stage] >= 3:
                    filled(act, "T", stage, u - 3)
                act.wait_ge(nb, u + 1)
                st = soft[:, u % 4, :]
                own.free(nc.scalar.activation(pbuf[:, u % 3, :], slot(("S", stage, u))[:, 0:TOK], ACT.Exp, bias=st[:, 1:2],
                                         scale=scale, accum_out=st[:, 2:3]), ev("S", stage, u))

            for g in range(2):
                split_high(("kv", g))
                for f in range(4):
                    v = filled(act, "q", g, f)
                    own(nc.scalar.activation(q_n[:, f, :], v[:, 0:SEQ], ACT.Copy), ev("q", g, f))
                for j in range(2):
                    v = filled(act, "q", g, 4 + j)
                    own(nc.scalar.activation(q_r[:, j, :], v[:, 0:SEQ], ACT.Copy), ev("q", g, 4 + j))
                for f in range(4):
                    v = filled(act, "kv", g, f)
                    own(nc.scalar.activation(k_n[:, f, :], v[:, 0:TOK], ACT.Copy), ev("kv", g, f))
                for m in range(NT):
                    v = filled(act, "v", g, m)
                    own(nc.scalar.activation(v_o[:, m, :], v[:, 0:512], ACT.Copy), ev("v", g, m))
                split_high(("kv", 1) if g == 0 else ("oout", "o"))
                exps("odd", 16 * g, po, s_nbo, O_SCALE)
                exps("odd", 16 * g + 1, po, s_nbo, O_SCALE)
                for u in range(16 * g, 16 * g + 16):
                    v = filled(act, "T", "odd", u)
                    if u % 16 >= 2:
                        filled(act, "O", "odd", u - 2)
                    own(nc.scalar.activation(ptb[u % 2][:], v[:, 0:TOK], ACT.Copy), ev("T", "odd", u))
                    if u % 16 < 14:
                        exps("odd", u + 2, po, s_nbo, O_SCALE)
            v = filled(act, "gate", 1, 0)
            own(nc.scalar.activation(gate_rows[:, 0, :], v, ACT.Copy), ev("gate", 1, 0))

            def mix_high(stage):
                for kt in range(KT):
                    v = filled(act, "mix", stage, kt)
                    own(nc.scalar.activation(xth[:, kt, CTX:TOK], v[:, 0:SEQ], ACT.Copy), s_xhi)

            mix_high("odd")
            split_high(("oout", "p"))
            split_high(("second", "qa"))
            squares(range(CT, NT), s_h2, lambda m: LT + m - CT + 1)
            squares(range(CT, NT), s_first, lambda m: m - CT + 1)
            squares(range(CT), s_ctx2, lambda m: 16 * CT)
            norm_high("second")
            for what, tiles, dst, func, nxt in (
                    ("qa", range(CT, NT), lambda m: qa[:, m - CT, :], ACT.Copy, ("second", "kk")),
                    ("kk", range(NT), lambda m: kk[:, m, :], ACT.Copy, ("second", "vr")),
                    ("vr", range(NT), lambda m: vr[:, m, :], ACT.Copy, ("second", "gr")),
                    ("gr", range(CT, NT), lambda m: gr[:, m - CT, :], ACT.Silu, ("second", "qr")),
                    ("qr", range(CT, NT), lambda m: qr[:, m - CT, :], ACT.Copy, ("sout", "o"))):
                split_high(nxt)
                for m in tiles:
                    v = filled(act, "second", what, m)
                    own(nc.scalar.activation(dst(m), v[:, 0:256 if what == "qr" else 512], func), ev("second", what, m))
            act.wait_ge(s_lg, 1)
            own(nc.scalar.activation(lg, lg, ACT.Exp, scale=-1.0), s_lge)
            for kt in range(4):
                v = filled(act, "turn", "qa", kt)
                own(nc.scalar.activation(qa_t[:, kt, :], v[:, 0:SEQ], ACT.Copy), ev("turn", "qa", kt))
            v = filled(act, "turn", "ka", 0)
            own(nc.scalar.activation(ka_t[:], v[:, 0:TOK], ACT.Copy), ev("turn", "ka", 0))
            for kt in range(2):
                v = filled(act, "turn", "qr2", kt)
                own(nc.scalar.activation(qr_t[:, kt, :], v[:, 0:SEQ], ACT.Copy), ev("turn", "qr2", kt))
                v = filled(act, "turn", "kr2", kt)
                own(nc.scalar.activation(kr2_t[:, kt, :], v[:, 0:TOK], ACT.Copy), ev("turn", "kr2", kt))
            v = filled(act, "gate", 2, 0)
            own(nc.scalar.activation(gate_rows[:, 0, :], v, ACT.Copy), ev("gate", 2, 0))
            exps("gqa", 0, pg, s_nbg, S_SCALE)
            exps("gqa", 1, pg, s_nbg, S_SCALE)
            for u in range(S_UNITS):
                if u % 2 == 0:
                    v = filled(act, "T", "gqa", u)
                    if u >= 2:
                        filled(act, "O", "gqa", u - 2)
                    own.free(nc.scalar.activation(ptg[:, u % 2, :], v[:, 0:TOK], ACT.Copy), ev("T", "gqa", u))
                if u + 2 < S_UNITS:
                    exps("gqa", u + 2, pg, s_nbg, S_SCALE)
            for h in range(R_HEADS):
                act.wait_ge(s_arg, h + 1)
                own(nc.scalar.activation(w_lat[:], w_lat[:], ACT.Exp), s_wl)
                far = dist[:, 512:R_TABLE]
                own(nc.scalar.activation(w_ctx[:], far, ACT.Exp, scale=lg[:, h:h + 1]))
                own(nc.scalar.activation(tmp[:, 0, 0:640], far, ACT.Exp, scale=lgt[:, 1:2], bias=lgt[:, 2:3]), s_wc)
            mix_high("second")
            split_high(("sout", "p"))

            squares(range(CT, NT), s_h3, lambda m: LT + m - CT + 1)
            for i in range(2):
                v = filled(act, "gate", 2, 1 + i)
                own(nc.scalar.activation(gate_rows[:, i, :], v, ACT.Copy), ev("gate", 2, 1 + i))
            for m in range(LT):
                act.wait_ge(s_row2, m + 1)
                own.free(nc.scalar.activation(h2h[:, m, :], h2[:, m, :], ACT.Copy), s_h2h)
            for kt in range(KT):
                v = filled(act, "turn", "h2", kt)
                own.free(nc.scalar.activation(h2_t[:, kt, :], v[:, 0:SEQ], ACT.Copy), ev("turn", "h2", kt))
            def high(j, i):
                act.wait_ge(s_ew[i % RAW], 32 * j + 16 * (i // RAW + 1))
                act.wait_ge(s_used, PARTS * j + i + 1)
                nc.scalar.activation(weh[i], raw[:, i % RAW, :], ACT.Copy).then_inc(s_eh, 1)

            def gathered(j):
                for h in range(2):
                    act.wait_ge(s_gat, 2 * j + h + 1)
                    nc.scalar.activation(xe_rows[:, 512 * h:512 * h + 512], ps[:, h, :], ACT.Copy).then_inc(s_rows, 1)

            def turned(j):
                for h in range(2):
                    act.wait_ge(s_turned, 2 * j + h + 1)
                    nc.scalar.activation(xeh[:, 4 * h:4 * h + 4, :], ps[:, 2 + h, :].rearrange("p (k n) -> p k n", k=4),
                                         ACT.Copy).then_inc(s_xeh, 1)

            def block_of(j, nxt):
                act.wait_ge(s_used, PARTS * j + 2 + PARTS)
                nc.scalar.activation(hid[:], ps[:, 4, :], ACT.Silu).then_inc(s_silu, 1)
                if nxt:
                    high(j + 1, 0)
                    high(j + 1, 1)
                    high(j + 1, 2)
                act.wait_ge(s_tr, j + 1)
                nc.scalar.activation(hth[:], ps[:, 4, :].rearrange("p (k n) -> p k n", k=4), ACT.Copy).then_inc(s_hth, 1)
                if nxt:
                    gathered(j + 1)
                    high(j + 1, 3)
                    turned(j + 1)
                    high(j + 1, 4)
                act.wait_ge(s_used, PARTS * j + 6 + PARTS)
                act.wait_ge(s_yst, 16 * j + 16)
                nc.scalar.activation(y_rows, slot_at(3), ACT.Copy).then_inc(s_yev, 1)
                if nxt:
                    high(j + 1, 5)

            nc.scalar.activation(route[:, 29:30], half[:, 0:1], ACT.Copy).then_inc(s_hth, 1)
            nc.scalar.activation(route[:, 30:31], half[:, 0:1], ACT.Copy).then_inc(s_yev, 1)
            for i in range(PARTS):
                high(0, i)
                if i == 3:
                    act.wait_ge(s_gd, 1)
                    nc.scalar.activation(route[:, 0:20], route[:, 0:20], ACT.Exp).then_inc(s_ge, 1)
            act.wait_ge(s_blocks, 1)
            last = act.value_load(blocks_i[0:1, 40:41], min_val=7, max_val=BLOCKS - 1)
            gathered(0)
            turned(0)
            with act.Fori(0, last) as j:
                block_of(j, True)
            block_of(last, False)
            for m in range(LT):
                act.wait_ge(s_x4, m + 1)
                for h in range(2):
                    own(nc.scalar.activation(junk, h_rows[:, CT + m, 512 * h:512 * h + 512], ACT.Square,
                                             accum_out=ss2[:, h, CT + m:CT + m + 1]), s_sq)

        @block.vector
        def _(dve):
            own = Own(dve, s_dve)
            made = [0]

            def split_low(upto):
                upto = upto if isinstance(upto, int) else plan.through[upto]
                while made[0] < min(upto, len(splits)):
                    k = made[0]
                    w = splits[k]["source"].shape[-1]
                    dve.wait_ge(s_hi, k + 1)
                    g = number[splits[k]["name"]]
                    own(nc.vector.tensor_tensor(wlo[:, k % SPLIT, 0:w], raw[:, g % RAW, 0:w],
                                                whi[:, k % SPLIT, 0:w].bitcast(F32), ALU.subtract), s_lo)
                    made[0] += 1
                    while g + 1 < len(pieces) and pieces[g + 1]["kind"] == "raw":
                        add_up(*pieces[g + 1]["name"][1:3])
                        g += 2

            summed = []

            def sums(w, layer, parts):
                for dst, cond in parts:
                    cv = cvec[:, 1 if layer == 2 else 0, :, cond]
                    own(nc.vector.tensor_scalar(dst, w[0][:, 0, :], cv[:, 0:1], None, ALU.mult))
                    for kt in range(1, KT):
                        ins = nc.vector.scalar_tensor_tensor(dst, w[kt // 4][:, kt % 4, :], cv[:, kt:kt + 1], dst,
                                                             ALU.mult, ALU.add)
                        if kt < KT - 1:
                            own(ins)
                return ins

            def add_up(layer, c):
                w = []
                for h in range(2):
                    g = number[("ada", layer, c, h)]
                    landed(dve, g)
                    w.append(raw[:, g % RAW, :].rearrange("p (k n) -> p k n", k=4))
                if with_context(layer, c):
                    before_this = [j for j in summed if with_context(*j)]
                    if before_this:
                        filled(dve, "ada", *before_this[-1])
                    own(sums(w, layer, ((acc[:], 0),)))
                    own(sums(w, layer, ((w[0][:, 0, :], 1),)), s_acc)
                else:
                    own(sums(w, layer, ((w[0][:, 0, :], 0),)), s_acc)
                summed.append((layer, c))

            def ada(layer, c):
                v = filled(dve, "ada", layer, c)
                n = 2 if with_context(layer, c) else 1
                b = vecs[:, VEC[f"ada{layer}"]][:, 4 * c:4 * c + 4].unsqueeze(2).broadcast_to([P, 4, n])
                own(nc.vector.tensor_tensor(mod[layer][:, 4 * c:4 * c + 4, 0:n],
                                            v[:, 0:8].rearrange("p (a b) -> p a b", b=2)[:, :, 0:n], b, ALU.add),
                    ev("ada", layer, c))

            def xt_low(stage, kt, source):
                dve.wait_ge(s_xhi, plan.xt[stage] + 1)
                return nc.vector.tensor_tensor(xtl[:, kt, :], source, xth[:, kt, :].bitcast(F32), ALU.subtract)

            def modulate(stage, layer, kt):
                v = filled(dve, "norm", stage, kt)
                sh = mod[layer][:, kt, :]
                own(nc.vector.tensor_scalar(tmp[:, kt % 2, CTX:TOK], v[:, 0:SEQ], scale_t[:, kt, 0:1], sh[:, 0:1],
                                            ALU.mult, ALU.add))
                own(nc.vector.tensor_scalar(tmp[:, kt % 2, 0:CTX], v[:, SEQ:TOK], scale_t[:, kt, 1:2], sh[:, 1:2],
                                        ALU.mult, ALU.add), ev("norm", stage, kt))

            def norm(stage, layer):
                nw = vecs[:, VEC[f"norm{layer}"]].unsqueeze(2).broadcast_to([P, KT, 2])
                evacuated(dve, "ada", layer, 3)
                own(nc.vector.scalar_tensor_tensor(scale_t[:], mod[layer][:, KT:2 * KT, :], 1.0, nw, ALU.add, ALU.mult))
                modulate(stage, layer, 0)
                for kt in range(KT):
                    if kt + 1 < KT:
                        modulate(stage, layer, kt + 1)
                    evacuated(dve, "norm", stage, kt)
                    own(xt_low(("norm", stage, kt), kt, tmp[:, kt % 2, :]), s_xlo)

            dve.wait_ge(s_const, 32)
            dve.wait_ge(s_cvec, 1)
            for c in (2, 3):
                dve.wait_ge(s_early[c], 32)
                w = [early[:, 2 * c + h, :].rearrange("p (k n) -> p k n", k=4) for h in range(2)]
                own(sums(w, 0, ((ao[:, c, :], 0),)))
                own(sums(w, 0, ((w[0][:, 0, :], 1),)), s_acc0)
            dve.wait_ge(s_const2, 16 * 8)
            pr = tmp[:, 0, 0:128].rearrange("p (a b) -> p a b", a=2)
            own(nc.vector.tensor_tensor(pr, lamv[:, 0:4:2, :], lamv[:, 1:4:2, :], ALU.mult))
            own(nc.vector.tensor_reduce(lam2, pr, AX, ALU.add), s_lam0)
            dve.wait_ge(s_lam0, 1)
            for c in range(4):
                ada(0, c)
            split_low(2)
            norm("even", 0)
            split_low(4)
            for m in range(NT):
                evacuated(dve, "even", "av", m)
                own(nc.vector.bn_stats(bn[:, 6 * m:6 * m + 6], vv[:, m, :]))
                own(nc.vector.bn_aggr(mv[:, 2 * m:2 * m + 2], bn[:, 6 * m:6 * m + 6]), s_ag)
                dve.wait_ge(s_ag, m + 1)
            ada(0, 4)
            split_low(6)
            dve.wait_ge(s_lnr, 1)
            for m in range(NT):
                own(nc.vector.tensor_scalar(vv[:, m, :], vv[:, m, :], mv[:, 2 * m:2 * m + 1], mv[:, 2 * m + 1:2 * m + 2],
                                            ALU.subtract, ALU.mult))
                own(nc.vector.tensor_tensor(vv[:, m, :], vv[:, m, :], ln_w[:], ALU.mult))
                own(nc.vector.tensor_tensor(vv[:, m, :], vv[:, m, :], ln_b[:], ALU.add))
            ada(0, 5)
            split_low(8)
            for m in range(NT):
                evacuated(dve, "even", "au", m)
                evacuated(dve, "even", "az", m)
                own(nc.vector.tensor_tensor(ao[:, m, :], ao[:, m, :], tmp[:, m % 2, 0:512], ALU.mult), s_vn)
            ada(1, 0)
            split_low(10)
            dve.wait_ge(s_vn, NT)
            bs = vecs[:, VEC["spatial_b"]]
            for g in range(8):
                v = filled(dve, "spatial", g)
                a = ao[:, :, 64 * g:64 * g + 64]
                own(nc.vector.scalar_tensor_tensor(a, v[:, 0:64 * NT].rearrange("p (n d) -> p n d", d=64), bs[:, g:g + 1],
                                               a, ALU.add, ALU.mult), ev("spatial", g))
            dve.wait_ge(s_lam1, 1)
            own(nc.vector.tensor_scalar(nlam, lam2[:, 1:2], lam2[:, 0:1], LAM_INIT, ALU.subtract, ALU.subtract))
            own(nc.vector.tensor_scalar(subln[:], subln[:], 1.0 - LAM_INIT, None, ALU.mult))
            ada(1, 1)
            split_low(12)
            for i, (what, dst, ready) in enumerate((("q", qt, s_q), ("k", kt_, s_k))):
                ada(1, 2 + i)
                split_low(14 + 2 * i)
                if i == 0:
                    for n in range(2):
                        dve.wait_ge(s_z[n], 16 * 3)
                for f in range(4):
                    v = filled(dve, "rope", what, f)
                    lat = dst[:, f, CTX:TOK]
                    own(nc.vector.tensor_tensor(tmp[:, f % 2, 0:SEQ], v[:, 0:SEQ], sin_t[:], ALU.mult), ev("rope", what, f))
                    own(nc.vector.tensor_tensor(lat, lat, cos_t[:], ALU.mult))
                    evacuated(dve, "rope", what, f)
                    own(nc.vector.tensor_tensor(lat, lat, tmp[:, f % 2, 0:SEQ], ALU.add), ready)
            for kt in range(4):
                v = filled(dve, "mix", "a", kt)
                own(xt_low(("mix", "a", kt), kt, v[:, 0:TOK]), ev("mix", "a", kt))

            def maxima(u):
                st = soft[:, u % 4, :]
                n = keys(u // 4)
                for i in range(2):
                    v = filled(dve, "S", "even", u, i)
                    own(nc.vector.tensor_reduce(st[:, i:i + 1], v[:, 0:n], AX, ALU.max))
                    own(nc.vector.tensor_scalar(st[:, 2 + i:3 + i], st[:, i:i + 1], -E_SCALE, None, ALU.mult), s_nb)

            def combine(u):
                st = soft[:, u % 4, :]
                n = keys(u // 4)
                evacuated(dve, "S", "even", u, 0)
                evacuated(dve, "S", "even", u, 1)
                own(nc.vector.reciprocal(st[:, 6:8], st[:, 4:6]))
                own(nc.vector.tensor_scalar(st[:, 7:8], st[:, 7:8], nlam, None, ALU.mult))
                own(nc.vector.tensor_scalar(p1[:, u % 2, 0:n], p1[:, u % 2, 0:n], st[:, 7:8], None, ALU.mult))
                own(nc.vector.scalar_tensor_tensor(p0[:, u % 3, 0:n], p0[:, u % 3, 0:n], st[:, 6:7], p1[:, u % 2, 0:n],
                                               ALU.mult, ALU.add), s_comb)

            def squares(m):
                t = tmp[:, 0, 0:512]
                own(nc.vector.tensor_tensor(t, o_rows[:, m, :], o_rows[:, m, :], ALU.mult))
                own(nc.vector.tensor_reduce(oss[:, 4 * m:4 * m + 4], t.rearrange("p (h d) -> p h d", d=P), AX, ALU.add), s_oss)

            def post(m):
                o = o_rows[:, m, :].rearrange("p (h d) -> p h d", d=P)
                dve.wait_ge(s_ors, m + 1)
                own(nc.vector.tensor_tensor(o, o, orstd[:, 4 * m:4 * m + 4].unsqueeze(2).broadcast_to([P, 4, P]), ALU.mult))
                own(nc.vector.tensor_tensor(o, o, subln[:].unsqueeze(1).broadcast_to([P, 4, P]), ALU.mult))
                dve.wait_ge(s_zin, 16 * (m + 1))
                own(nc.vector.tensor_tensor(o_rows[:, m, :], o_rows[:, m, :], z_in[:], ALU.mult), s_post)

            maxima(0)
            maxima(1)
            combine(0)
            for u in range(E_UNITS):
                if u + 1 < E_UNITS:
                    combine(u + 1)
                if u % 4 == 0 and u:
                    post(u // 4 - 1)
                if u + 2 < E_UNITS:
                    maxima(u + 2)
                v = filled(dve, "O", "even", u)
                own(nc.vector.tensor_copy(o_rows[:, u // 4, P * (u % 4):P * (u % 4) + P], v[:, 0:P]), ev("O", "even", u))
                if u % 4 == 3:
                    for h in range(4):
                        evacuated(dve, "O", "even", u - 3 + h)
                    squares(u // 4)
            post(NT - 1)
            for kt in range(4, 8):
                v = filled(dve, "mix", "b", kt)
                own(xt_low(("mix", "b", kt), kt, v[:, 0:TOK]), ev("mix", "b", kt))
            dve.wait_ge(s_xr, 16 * NT)
            for c, what in enumerate("op"):
                split_low(2 * (7 + c + 2))
                for m in range(NT):
                    v = filled(dve, "eout", what, m)
                    g = gate_rows[:, 0 if m >= CT else 1, 512 * c:512 * c + 512]
                    own(nc.vector.tensor_tensor(tmp[:, m % 2, 0:512], v[:, 0:512], g, ALU.mult), ev("eout", what, m))
                    evacuated(dve, "eout", what, m)
                    h = h_rows[:, m, 512 * c:512 * c + 512]
                    own(nc.vector.tensor_tensor(h, h, tmp[:, m % 2, 0:512], ALU.add), s_h)
                ada(1, 4 + c)

            def normalise(tiles, ready, count, stored, total):
                dve.wait_ge(ready, count)
                dve.wait_ge(stored, total)
                for m in tiles:
                    own.free(nc.vector.tensor_scalar(h_rows[:, m, :], h_rows[:, m, :], rstd[:, m:m + 1], None, ALU.mult),
                             s_xn2)
                own.wait()

            normalise(range(NT), s_rs2, 1, s_spill, 16 * LT)
            split_low(("odd", "a"))
            norm("odd", 1)
            split_low(("odd", "z"))
            for m in range(NT):
                evacuated(dve, "odd", "a", m)
                t = tmp[:, 0, 0:384]
                own(nc.vector.tensor_tensor(t, a_rows[:, m, 0:384], a_rows[:, m, 0:384], ALU.mult))
                own(nc.vector.tensor_reduce(osum[:, m:m + 1], t[:, 0:256], AX, ALU.add))
                own(nc.vector.tensor_reduce(osum[:, 6 + m:7 + m], t[:, 256:384], AX, ALU.add), s_ao)
            ada(2, 0)
            dve.wait_ge(s_cp, 2)
            for m in range(NT):
                if m >= CT:
                    own(nc.vector.tensor_scalar(a_rows[:, m, 0:256], a_rows[:, m, 0:256], osum[:, 12 + m:13 + m], None,
                                                ALU.mult))
                own(nc.vector.tensor_scalar(a_rows[:, m, 256:384], a_rows[:, m, 256:384], osum[:, 18 + m:19 + m], None,
                                            ALU.mult), s_cn)
            split_low(("odd", "y"))
            qn, kvn = vecs[:, VEC["q_norm"]], vecs[:, VEC["kv_norm"]]
            for kt in range(2):
                v = filled(dve, "turn", "cq", kt)
                own(nc.vector.tensor_scalar(cq_f[:, kt, :], v[:, 0:SEQ], qn[:, kt:kt + 1], None,
                                            ALU.mult), ev("turn", "cq", kt))
            v = filled(dve, "turn", "ckv", 0)
            own(nc.vector.tensor_scalar(ckv_f[:], v[:, 0:TOK], kvn, None, ALU.mult), ev("turn", "ckv", 0))
            split_low(("q", 0))
            for kt in range(2):
                dve.wait_ge(s_ct_hi, kt + 1)
                own(nc.vector.tensor_tensor(cql[:, kt, :], cq_f[:, kt, :],
                                            cqh[:, kt, :].bitcast(F32), ALU.subtract), s_ct_lo)
            dve.wait_ge(s_ct_hi, 3)
            own(nc.vector.tensor_tensor(ckvl[:], ckv_f[:], ckvh[:].bitcast(F32), ALU.subtract), s_ct_lo)

            def rotate(job, lat, t, ready):
                v = filled(dve, *job)
                own(nc.vector.tensor_tensor(t, v[:, 0:SEQ], sin_t[:], ALU.mult), ev(*job))
                own(nc.vector.tensor_tensor(lat, lat, cos_t[:], ALU.mult))
                own(nc.vector.tensor_tensor(lat, lat, t, ALU.add), ready)

            rotate(("rope", "kr", 0), kr_t[:, CTX:TOK], cq_f[:, 0, :], s_kr)
            ada(2, 1)

            def maximum(stage, u, nb, scale):
                st = soft[:, u % 4, :]
                v = filled(dve, "S", stage, u)
                own(nc.vector.tensor_reduce(st[:, 0:1], v[:, 0:TOK], AX, ALU.max))
                own(nc.vector.tensor_scalar(st[:, 1:2], st[:, 0:1], -scale, None, ALU.mult), nb)

            def scaled_out(stage, u, dst, n):
                st = soft[:, u % 4, :]
                evacuated(dve, "S", stage, u)
                own(nc.vector.reciprocal(st[:, 3:4], st[:, 2:3]))
                v = filled(dve, "O", stage, u)
                own(nc.vector.tensor_scalar(dst, v[:, 0:n], st[:, 3:4], None, ALU.mult), ev("O", stage, u))

            for i in range(2):
                dve.wait_ge(s_y[i], 16 * 4)
            ada(2, 2)
            for g in range(2):
                split_low(("kv", g))
                for j in range(2):
                    rotate(("rope", "qr", 2 * g + j), q_r[:, j, :], tmp[:, 0, 0:SEQ], s_qr)
                split_low(("kv", 1) if g == 0 else ("oout", "o"))
                maximum("odd", 16 * g, s_nbo, O_SCALE)
                maximum("odd", 16 * g + 1, s_nbo, O_SCALE)
                for u in range(16 * g, 16 * g + 16):
                    if u % 16 < 14:
                        maximum("odd", u + 2, s_nbo, O_SCALE)
                    m, h = u % 16 // 4, 4 * g + u % 4
                    scaled_out("odd", u, oo_rows[:, m, P * h:P * h + P], P)
                    if g == 1 and u % 4 == 3:
                        dve.wait_ge(s_yin[m % 2], 16 * (m // 2 + 1))
                        own(nc.vector.tensor_tensor(oo_rows[:, m, :], oo_rows[:, m, :], y_in[:, m % 2, :], ALU.mult), s_oy)
                ada(2, 3 + g)

            def mix_low(stage):
                for kt in range(KT):
                    v = filled(dve, "mix", stage, kt)
                    dve.wait_ge(s_xhi, plan.xt[("mix", stage, kt)] + 1)
                    own(nc.vector.tensor_tensor(xtl[:, kt, CTX:TOK], v[:, 0:SEQ], xth[:, kt, CTX:TOK].bitcast(F32),
                                                ALU.subtract), ev("mix", stage, kt))

            def add_out(stage, loaded, ready, nexts):
                dve.wait_ge(loaded, 16 * LT)
                for c, what in enumerate("op"):
                    split_low(nexts[c])
                    for m in range(CT, NT):
                        v = filled(dve, stage, what, m)
                        own(nc.vector.tensor_tensor(tmp[:, m % 2, 0:512], v[:, 0:512],
                                                    gate_rows[:, 0, 512 * c:512 * c + 512], ALU.mult), ev(stage, what, m))
                        h = h_rows[:, m, 512 * c:512 * c + 512]
                        own(nc.vector.tensor_tensor(h, h, tmp[:, m % 2, 0:512], ALU.add), ready)
                    if stage == "oout":
                        ada(2, 5 + c)

            mix_low("odd")
            evacuated(dve, "gate", 1, 0)
            add_out("oout", s_hr, s_h2, (("oout", "p"), ("second", "qa")))
            dve.wait_ge(s_rs2, 2)
            dve.wait_ge(s_fw, 16)
            for m in range(CT, NT):
                own(nc.vector.tensor_scalar(h_rows[:, m, :], h_rows[:, m, :], rstd[:, m:m + 1], None, ALU.mult))
                own(nc.vector.tensor_tensor(h_rows[:, m, :], h_rows[:, m, :], final_w[:], ALU.mult), s_first)
            normalise(range(NT), s_rs2, 3, s_x2st, 16 * LT)
            norm("second", 2)

            def spin(x, heads, m, t, ready=None):
                c = cos_t[:, 64 * m:64 * m + 64].rearrange("p (f e) -> p f e", e=2)
                s = sin_t[:, 64 * m:64 * m + 64].rearrange("p (f e) -> p f e", e=2)
                x = x.rearrange("p (h f e) -> p h f e", f=32, e=2)
                t = t.rearrange("p (h f e) -> p h f e", f=32, e=2)
                for e in range(2):
                    own(nc.vector.tensor_tensor(t[:, :, :, e], x[:, :, :, 1 - e],
                                                s[:, :, e].unsqueeze(1).broadcast_to([P, heads, 32]), ALU.mult))
                for e in range(2):
                    own(nc.vector.tensor_tensor(x[:, :, :, e], x[:, :, :, e],
                                                c[:, :, e].unsqueeze(1).broadcast_to([P, heads, 32]), ALU.mult))
                    own(nc.vector.tensor_tensor(x[:, :, :, e], x[:, :, :, e], t[:, :, :, e], ALU.add), ready if e else None)

            def head_squares(x, heads, to):
                t = tmp[:, 0, 0:64 * heads]
                own(nc.vector.tensor_tensor(t, x, x, ALU.mult))
                own(nc.vector.tensor_reduce(to, t.rearrange("p (h d) -> p h d", d=64), AX, ALU.add), s_sn)

            def head_norm(x, heads, powers, which):
                x = x.rearrange("p (h d) -> p h d", d=64)
                own(nc.vector.tensor_tensor(x, x, powers.unsqueeze(2).broadcast_to([P, heads, 64]), ALU.mult))
                own(nc.vector.tensor_tensor(x, x, subln[:, 64 * which:64 * which + 64].unsqueeze(1)
                                            .broadcast_to([P, heads, 64]), ALU.mult))

            split_low(("second", "kk"))
            for m in range(LT):
                evacuated(dve, "second", "qa", CT + m)
                head_squares(qa[:, m, :], 8, osum[:, 8 * m:8 * m + 8])
            ada(2, 7)
            split_low(("second", "vr"))
            for m in range(NT):
                evacuated(dve, "second", "kk", m)
                head_squares(kk[:, m, 0:P], 2, osum[:, 32 + 2 * m:34 + 2 * m])
            ada(2, 8)
            split_low(("second", "gr"))
            dve.wait_ge(s_rt, 16 * 3)
            dve.wait_ge(s_sp, 1)
            for m in range(LT):
                head_norm(qa[:, m, :], 8, osum[:, 8 * m:8 * m + 8], 0)
                spin(qa[:, m, :], 8, m, tmp[:, 0, 0:512])
            ada(2, 9)
            split_low(("second", "qr"))
            for m in range(NT):
                head_norm(kk[:, m, 0:P], 2, osum[:, 32 + 2 * m:34 + 2 * m], 1)
                if m >= CT:
                    spin(kk[:, m, 0:P], 2, m - CT, tmp[:, 0, 0:P])
                    spin(kk[:, m, 256:512], 4, m - CT, tmp[:, 0, 0:256])
            ada(2, 10)
            for m in range(LT):
                evacuated(dve, "second", "qr", CT + m)
                spin(qr[:, m, :], 4, m, tmp[:, 0, 0:256], s_qn)
            split_low(("sout", "o"))
            dec = vecs[:, VEC["decay"]]
            own(nc.vector.tensor_scalar(lg, dec, -1.0, None, ALU.mult))
            own(nc.vector.tensor_tensor(lg, lg, dec, ALU.max), s_lg)
            dve.wait_ge(s_lge, 1)
            a, b, c = rstats[:, 0:8], rstats[:, 8:16], rstats[:, 16:24]
            own(nc.vector.tensor_scalar(a, lg, 2.0, None, ALU.add))
            own(nc.vector.reciprocal(a, a))
            own(nc.vector.tensor_tensor(a, a, lg, ALU.mult))
            own(nc.vector.tensor_tensor(b, a, a, ALU.mult))
            own(nc.vector.memset(c, 1.0 / 17))
            for n in (15, 13, 11, 9, 7, 5, 3, 1):
                own(nc.vector.tensor_tensor(c, c, b, ALU.mult))
                own(nc.vector.tensor_scalar(c, c, 1.0 / n, None, ALU.add))
            own(nc.vector.tensor_tensor(c, c, a, ALU.mult))
            own(nc.vector.tensor_scalar(a, dec, 0.0, None, ALU.min))
            own(nc.vector.scalar_tensor_tensor(lg, c, -2.0, a, ALU.mult, ALU.add))

            ada(2, 11)
            maximum("gqa", 0, s_nbg, S_SCALE)
            maximum("gqa", 1, s_nbg, S_SCALE)
            for u in range(S_UNITS):
                if u % 2:
                    v = filled(dve, "T", "gqa", u)
                    if u >= 2:
                        filled(dve, "O", "gqa", u - 2)
                    own.free(nc.vector.tensor_copy(ptg[:, u % 2, :], v[:, 0:TOK]), ev("T", "gqa", u))
                if u + 2 < S_UNITS:
                    maximum("gqa", u + 2, s_nbg, S_SCALE)
                m, h = u // 8, u % 8
                scaled_out("gqa", u, oa_rows[:, m, 64 * h:64 * h + 64], 64)
            dve.wait_ge(s_dist, 1)
            dve.wait_ge(s_gnl, 16)
            def decays(h):
                own.free(nc.vector.tensor_scalar(lgt[:, 1:2], lg[:, 4 + h:5 + h], -1.0, None, ALU.mult))
                own(nc.vector.tensor_scalar(lgt[:, 2:3], lg[:, 4 + h:5 + h], 768.0, None, ALU.mult))
                near = dist[:, 0:896]
                own.free(nc.vector.tensor_scalar(w_lat[:], near, 0.0, lg[:, h:h + 1], ALU.max, ALU.mult))
                t = tmp[:, :, :].rearrange("p a b -> p (a b)")[:, 0:896]
                own(nc.vector.tensor_scalar(t, near, 0.0, lgt[:, 1:2], ALU.min, ALU.mult))
                own(nc.vector.tensor_tensor(w_lat[:], w_lat[:], t, ALU.add), s_arg)

            def decayed(h):
                dve.wait_ge(s_wc, h + 1)
                own(nc.vector.tensor_tensor(w_ctx[:], w_ctx[:], tmp[:, 0, 0:640], ALU.add))
                if h:
                    filled(dve, "RO", h - 1)
                for a in range(NT):
                    v = filled(dve, "R", h, a)
                    w = w_ctx[:, 128 * (1 - a):128 * (1 - a) + SEQ] if a < CT else \
                        w_lat[:, 384 - 128 * (a - CT):384 - 128 * (a - CT) + SEQ]
                    own.free(nc.vector.scalar_tensor_tensor(sw[:, a, :], v[:, 0:SEQ], 64 ** -0.5, w, ALU.mult, ALU.mult),
                             ev("R", h, a))
                own.wait()

            def read_out(h):
                v = filled(dve, "RO", h)
                o = or_rows[:, :, P * h:P * h + P]
                own(nc.vector.tensor_copy(o, v[:, 0:SEQ].rearrange("p (m d) -> p m d", d=P)), ev("RO", h))
                for m in range(LT):
                    own.free(nc.vector.bn_stats(oss[:, 6 * m:6 * m + 6], o[:, m, :]))
                own.wait()
                for m in range(LT):
                    own.free(nc.vector.bn_aggr(rstats[:, 8 * h + 2 * m:8 * h + 2 * m + 2], oss[:, 6 * m:6 * m + 6]), s_gs)
                own.wait()

            def normed(h):
                o = or_rows[:, :, P * h:P * h + P]
                dve.wait_ge(s_gp, h + 1)
                for m in range(LT):
                    r = rstats[:, 8 * h + 2 * m:8 * h + 2 * m + 2]
                    own.free(nc.vector.tensor_scalar(o[:, m, :], o[:, m, :], r[:, 0:1], r[:, 1:2], ALU.subtract, ALU.mult))
                own.wait()
                for i, op in ((0, ALU.mult), (1, ALU.add)):
                    own(nc.vector.tensor_tensor(o, o, gn[:, i, P * h:P * h + P].unsqueeze(1).broadcast_to([P, LT, P]), op))
                own(nc.vector.tensor_tensor(o, o, gr[:, :, P * h:P * h + P], ALU.mult), s_ret)

            decays(0)
            decayed(0)
            for h in range(R_HEADS):
                if h + 1 < R_HEADS:
                    decays(h + 1)
                read_out(h)
                if h + 1 < R_HEADS:
                    decayed(h + 1)
                normed(h)
            mix_low("second")
            evacuated(dve, "gate", 2, 0)
            add_out("sout", s_h3r, s_h3, (("sout", "p"), ("sout", "p")))

            dve.wait_ge(s_rcl, 48)
            m2 = mod[2][:, 4 * KT:5 * KT, 0]
            own(nc.vector.scalar_tensor_tensor(m2, m2, 1.0, vecs[:, VEC["norm2"]], ALU.add, ALU.mult), s_mods)
            nc.vector.tensor_copy(route[:, 27:28], half[:, 0:1]).then_inc(s_el, RAW)
            v = filled(dve, "free", 0)
            own(nc.vector.tensor_copy(route[:, 31:32], v[:, 0:1]), ev("free", 0))
            dve.wait_ge(s_rs2, 4)
            for i in range(2):
                evacuated(dve, "gate", 2, 1 + i)
            for m in range(LT):
                own(nc.vector.scalar_tensor_tensor(h2[:, m, :], h_rows[:, CT + m, :], rstd[:, CT + m:CT + m + 1],
                                                   gate_rows[:, 0, :], ALU.mult, ALU.mult))
                own(nc.vector.tensor_tensor(h2[:, m, :], h2[:, m, :], gate_rows[:, 1, :], ALU.add), s_row2)
            for m in range(LT):
                dve.wait_ge(s_h2h, m + 1)
                own.free(nc.vector.tensor_tensor(h2l[:, m, :], h2[:, m, :], h2h[:, m, :].bitcast(F32), ALU.subtract), s_h2l)

            def low(j, i):
                dve.wait_ge(s_eh, PARTS * j + i + 1)
                nc.vector.tensor_tensor(wel[i], raw[:, i % RAW, :], weh[i].bitcast(F32), ALU.subtract).then_inc(s_el, 1)

            for i in range(SPLIT):
                low(0, i)

            v = filled(dve, "router")
            logits = tmp[:, 0, 0:144].rearrange("p (m n) -> p m n", m=LT)
            grp, ex = logits[:, :, 0:4], logits[:, :, 4:36]
            pick = tmp[:, 0, 144:160].rearrange("p (m n) -> p m n", m=LT)
            chosen = [tmp[:, 0, 160 + 128 * i:288 + 128 * i].rearrange("p (m n) -> p m n", m=LT) for i in range(2)]
            work = tmp[:, 0, 416:544].rearrange("p (m n) -> p m n", m=LT)
            both = tmp[:, 0, 544:672].rearrange("p (m n) -> p m n", m=LT)
            top = [tmp[:, 0, 672 + 4 * i:676 + 4 * i] for i in range(4)]

            def over(x, n):
                return x.unsqueeze(2).broadcast_to([P, LT, n])

            def first_of_max(dst, x, n, best):
                own(nc.vector.tensor_reduce(best, x, AX, ALU.max))
                own(nc.vector.tensor_tensor(dst, x, over(best, n), ALU.is_ge))
                own(nc.vector.tensor_tensor(dst, dst, falling[:, 32 - n:32].unsqueeze(1).broadcast_to([P, LT, n]), ALU.mult))
                own(nc.vector.tensor_reduce(top[3], dst, AX, ALU.max))
                own(nc.vector.tensor_tensor(dst, dst, over(top[3], n), ALU.is_equal))

            own(nc.vector.tensor_tensor(logits, v[:, 0:144].rearrange("p (m n) -> p m n", m=LT),
                                        router_b.unsqueeze(1).broadcast_to([P, LT, 36]), ALU.add), ev("router"))
            first_of_max(pick, grp, 4, top[0])
            own(nc.vector.tensor_tensor(route[:, 0:16].rearrange("p (m n) -> p m n", m=LT), grp, over(top[0], 4), ALU.subtract))
            own(nc.vector.tensor_scalar(pick, pick, 1.0, FAR, ALU.subtract, ALU.mult))
            for m in range(LT):
                x = ex[:, m, :].rearrange("p (g e) -> p g e", g=GROUPS)
                own(nc.vector.tensor_tensor(x, x, pick[:, m, :].unsqueeze(2).broadcast_to([P, GROUPS, 8]), ALU.add))
            first_of_max(chosen[0], ex, EXPERTS, top[1])
            own(nc.vector.scalar_tensor_tensor(ex, chosen[0], -FAR, ex, ALU.mult, ALU.add))
            first_of_max(chosen[1], ex, EXPERTS, top[2])
            own(nc.vector.tensor_tensor(both, chosen[0], chosen[1], ALU.add), s_chosen)
            own(nc.vector.tensor_tensor(route[:, 16:20], top[2], top[1], ALU.subtract), s_gd)
            v = filled(dve, "free", 1)
            own(nc.vector.tensor_copy(route[:, 31:32], v[:, 0:1]), ev("free", 1))
            v = filled(dve, "counts")
            need = route[:, 24:28]
            own(nc.vector.tensor_tensor(need[0:EXPERTS, :], thresholds[0:EXPERTS, :],
                                        v[0:EXPERTS, 512:513].broadcast_to([EXPERTS, 4]), ALU.is_lt))
            own(nc.vector.tensor_reduce(route[0:EXPERTS, 28:29], need[0:EXPERTS, :], AX, ALU.add))
            own(nc.vector.tensor_scalar(route[0:1, 28:29], route[0:1, 28:29], 1.0, None, ALU.max), s_nblk)
            s = filled(dve, "starts")
            first = tmp[:, 1, 0:33]
            own(nc.vector.tensor_copy(first, s[:, 0:33]), ev("starts"))
            own(nc.vector.scalar_tensor_tensor(work, first[:, 0:EXPERTS].unsqueeze(1).broadcast_to([P, LT, EXPERTS]), float(P),
                                               v[:, 0:128].rearrange("p (m n) -> p m n", m=LT), ALU.mult, ALU.add),
                ev("counts"))
            for c in range(2):
                own(nc.vector.tensor_tensor(chosen[c], chosen[c], work, ALU.mult))
                own(nc.vector.tensor_reduce(dest[:, 4 * c:4 * c + 4], chosen[c], AX, ALU.add))
            own(nc.vector.tensor_copy(dest_i, dest))
            nb = BLOCKS + 1
            at_b = tmp[:, 1, 40:40 + nb]
            own(nc.vector.tensor_scalar(at_b, block_first, 1.0 / P, None, ALU.mult))
            ends = raw[:, 0, 0:nb * EXPERTS].rearrange("p (b e) -> p b e", b=nb)
            own(nc.vector.tensor_tensor(ends, first[:, 1:33].unsqueeze(1).broadcast_to([P, nb, EXPERTS]),
                                        at_b.unsqueeze(2).broadcast_to([P, nb, EXPERTS]), ALU.is_le))
            own(nc.vector.tensor_reduce(at_b, ends, AX, ALU.add))
            own(nc.vector.tensor_scalar(at_b, at_b, EXPERTS - 1.0, None, ALU.min))
            own(nc.vector.tensor_copy(blocks_i[:, 0:nb], at_b))
            own(nc.vector.tensor_copy(blocks_i[:, 41:42], first[:, 32:33]))
            own(nc.vector.tensor_scalar(blocks_i[:, 42:43], first[:, 32:33], -1.0, BLOCKS + 1.0, ALU.mult, ALU.add))
            own(nc.vector.tensor_scalar(blocks_i[:, 40:41], first[:, 32:33], -1.0, None, ALU.add), s_blocks)
            rel = tmp[:, 1, 80:80 + 4 * nb].rearrange("p (b m) -> p b m", m=LT)
            ok = tmp[:, 1, 240:240 + 4 * nb].rearrange("p (b m) -> p b m", m=LT)
            wh = where.rearrange("p (b m) -> p b m", m=LT)
            for c in range(2):
                own(nc.vector.tensor_tensor(rel, dest[:, 4 * c:4 * c + 4].unsqueeze(1).broadcast_to([P, nb, LT]),
                                            block_first.unsqueeze(2).broadcast_to([P, nb, LT]), ALU.subtract))
                own(nc.vector.tensor_scalar(ok, rel, float(P), None, ALU.is_lt))
                own(nc.vector.scalar_tensor_tensor(ok, rel, 0.0, ok, ALU.is_ge, ALU.mult))
                if c == 0:
                    own(nc.vector.scalar_tensor_tensor(wh, rel, 1.0, ok, ALU.add, ALU.mult))
                else:
                    own(nc.vector.scalar_tensor_tensor(ok, rel, 1.0, ok, ALU.add, ALU.mult))
                    own(nc.vector.scalar_tensor_tensor(wh, wh, -1.0, ok, ALU.add, ALU.add))

            dve.wait_ge(s_ge, 1)
            own(nc.vector.tensor_reduce(route[:, 20:24], route[:, 0:16].rearrange("p (m n) -> p m n", m=LT), AX, ALU.add))
            own(nc.vector.scalar_tensor_tensor(route[:, 20:24], route[:, 16:20], 1.0, route[:, 20:24], ALU.add, ALU.mult))
            own(nc.vector.reciprocal(pair_w[:, 0:4], route[:, 20:24]))
            own(nc.vector.tensor_tensor(pair_w[:, 4:8], pair_w[:, 0:4], route[:, 16:20], ALU.mult), s_rw)
            dve.wait_ge(s_blocks, 1)
            last = dve.value_load(blocks_i[0:1, 40:41], min_val=7, max_val=BLOCKS - 1)

            def one_hot(j):
                for m in range(LT):
                    ins = nc.vector.tensor_scalar(hot[:, m, :], col, where[:, bass.ds(j * LT + m, 1)], None, ALU.is_equal)
                ins.then_inc(s_hot, 1)

            def turned(j):
                for h in range(2):
                    dve.wait_ge(s_xeh, 2 * j + h + 1)
                    at_h = slice(4 * h, 4 * h + 4)
                    nc.vector.tensor_tensor(xel[:, at_h, :], ps[:, 2 + h, :].rearrange("p (k n) -> p k n", k=4),
                                            xeh[:, at_h, :].bitcast(F32), ALU.subtract).then_inc(s_xel, 1)

            def block_of(j, nxt):
                if nxt:
                    dve.wait_ge(s_gat, 2 * j + 2)
                    one_hot(j + 1)
                    low(j + 1, 0)
                dve.wait_ge(s_silu, j + 1)
                dve.wait_ge(s_used, PARTS * j + 4 + PARTS)
                nc.vector.tensor_tensor(hid[:], hid[:], ps[:, 5, :], ALU.mult).then_inc(s_hid, 1)
                if nxt:
                    low(j + 1, 1)
                dve.wait_ge(s_hth, j + 2)
                nc.vector.tensor_tensor(htl[:], ps[:, 4, :].rearrange("p (k n) -> p k n", k=4), hth[:].bitcast(F32),
                                        ALU.subtract).then_inc(s_htl, 1)
                if nxt:
                    low(j + 1, 2)
                    low(j + 1, 3)
                    turned(j + 1)
                    low(j + 1, 4)
                    low(j + 1, 5)

            own.wait()
            nc.vector.tensor_copy(route[:, 28:29], half[:, 0:1]).then_inc(s_htl, 1)
            one_hot(0)
            for i in range(SPLIT, PARTS):
                low(0, i)
            turned(0)
            with dve.Fori(0, last) as j:
                block_of(j, True)
            block_of(last, False)

            v = filled(dve, "gate", 2, 3)
            own(nc.vector.tensor_copy(gt2[:], v), ev("gate", 2, 3))
            for m in range(LT):
                dve.wait_ge(s_pair[m], 32)
                y0, y1 = pairs[:, m, 0, :], pairs[:, m, 1, :]
                own(nc.vector.tensor_scalar(y0, y0, pair_w[:, m:m + 1], None, ALU.mult))
                own(nc.vector.scalar_tensor_tensor(y0, y1, pair_w[:, 4 + m:5 + m], y0, ALU.mult, ALU.add))
                own(nc.vector.tensor_tensor(y0, y0, gt2[:], ALU.mult))
                own(nc.vector.tensor_tensor(h_rows[:, CT + m, :], h_rows[:, CT + m, :], y0, ALU.add), s_x4)
            dve.wait_ge(s_fgl, 16)
            dve.wait_ge(s_rs2, 5)
            for m in range(LT):
                x = h_rows[:, CT + m, :]
                own.free(nc.vector.scalar_tensor_tensor(x, x, rstd[:, CT + m:CT + m + 1], final_g[:], ALU.mult, ALU.mult),
                         s_fin)

        @block.tensor
        def _(pe):
            order = iter(jobs)

            def begin(*job):
                assert next(order) == job, job
                n = jobs[job]
                if n >= SLOTS:
                    pe.wait_ge(s_ev[n % SLOTS], n // SLOTS)
                return slot(job)

            def end(ins, *job):
                ins.then_inc(s_mm[jobs[job] % SLOTS], 1)

            added = []

            def ada(layer, c):
                v = begin("ada", layer, c)
                if (layer, c) >= (0, 2):
                    if layer == 0 and c < 4:
                        pe.wait_ge(s_acc0, c - 1)
                        sums = (ao[:, c, :], early[:, 2 * c, 0:512])
                    else:
                        pe.wait_ge(s_acc, len(added) + 1)
                        added.append(c)
                        g = number[("ada", layer, c, 0)]
                        first = raw[:, g % RAW, 0:512]
                        sums = (acc[:], first) if with_context(layer, c) else (first,)
                    for f in range(4):
                        for cond, x in enumerate(sums):
                            mm = nc.tensor.matmul(v[:, 2 * f + cond:2 * f + cond + 1], x[:, P * f:P * f + P], half[:, 1:2],
                                                  start=True, stop=True)
                    end(mm, "ada", layer, c)
                    return
                pe.wait_ge(s_early[c], 32)
                w = [early[:, 2 * c + h, :].rearrange("p (k n) -> p k n", k=4) for h in range(2)]
                for f in range(4):
                    for kt in range(KT):
                        mm = nc.tensor.matmul(v[:, 2 * f:2 * f + 2], w[kt // 4][:, kt % 4, P * f:P * f + P],
                                              cvec[:, 1 if layer == 2 else 0, kt, :], start=kt == 0, stop=kt == KT - 1)
                end(mm, "ada", layer, c)

            def parts(layer, what, h, k=4):
                p = splits[pieces[number[(layer, what, h)]]["k"]]
                pe.wait_ge(s_lo, p["k"] + 1)
                i = p["k"] % SPLIT
                return (whi[:, i, :].rearrange("p (k n) -> p k n", k=k), wlo[:, i, :].rearrange("p (k n) -> p k n", k=k))

            def three(v, a, b, first, last):
                nc.tensor.matmul(v, a[0], b[0], start=first, stop=False)
                nc.tensor.matmul(v, a[0], b[1], start=False, stop=False)
                return nc.tensor.matmul(v, a[1], b[0], start=False, stop=last)

            def xt(kt, at):
                return xth[:, kt, at], xtl[:, kt, at]

            def rows(layer, what, tiles, n=512, made=None):
                w = [parts(layer, what, h) for h in range(2)]
                tiles = list(tiles)
                if made is not None:
                    two, tiles = tiles[0:2], tiles[2:]
                    v = {}
                    for m, kts in ((two[0], range(0, 6)), (two[1], range(0, 6)), (two[0], (6, 7)), (two[1], (6, 7))):
                        if m not in v:
                            v[m] = begin(layer, what, m)
                        for kt in kts:
                            pe.wait_ge(s_xlo, made + kt + 1)
                            wk = tuple(x[:, kt % 4, 0:n] for x in w[kt // 4])
                            mm = three(v[m][:, 0:n], xt(kt, slice(P * m, P * m + P)), wk, kt == 0, kt == KT - 1)
                        if kt == KT - 1:
                            end(mm, layer, what, m)
                for m in tiles:
                    v = begin(layer, what, m)
                    for kt in range(KT):
                        wk = tuple(x[:, kt % 4, 0:n] for x in w[kt // 4])
                        mm = three(v[:, 0:n], xt(kt, slice(P * m, P * m + P)), wk, kt == 0, kt == KT - 1)
                    end(mm, layer, what, m)

            def columns(layer, what):
                w = [parts(layer, what, h) for h in range(2)]
                for f in range(4):
                    v = begin(layer, what, f)
                    for to, at in ((slice(0, SEQ), slice(CTX, TOK)), (slice(SEQ, TOK), slice(0, CTX))):
                        for kt in range(KT):
                            wk = tuple(x[:, kt % 4, P * f:P * f + P] for x in w[kt // 4])
                            mm = three(v[:, to], wk, xt(kt, at), kt == 0, kt == KT - 1)
                    end(mm, layer, what, f)

            def turn(job, source, cols):
                v = begin(*job)
                for rows_, to in zip(source, cols):
                    mm = nc.tensor.transpose(v[:, to:to + P], rows_, ident[:])
                end(mm, *job)

            norm_cols = [SEQ + P * m for m in range(CT)] + [P * m for m in range(LT)]

            pe.wait_ge(s_cvec, 1)
            pe.wait_ge(s_half, 2)
            for c in range(4):
                ada(0, c)
            pe.wait_ge(s_const, 32)
            pe.wait_ge(s_const2, 16 * 8)
            pe.wait_ge(s_xn, NT)
            for kt in range(KT):
                turn(("norm", "even", kt), [h_rows[:, m, P * kt:P * kt + P] for m in range(NT)], norm_cols)
            tiles = range(NT)
            rows("even", "av", tiles, made=0)
            ada(0, 4)
            rows("even", "au", tiles)
            ada(0, 5)
            rows("even", "az", tiles)
            ada(1, 0)
            rows("even", "bv", tiles)
            pe.wait_ge(s_vn, NT)
            for g in range(8):
                v = begin("spatial", g)
                end(nc.tensor.matmul(v[:, 0:64 * NT].rearrange("p (n d) -> p n d", d=64), spatial_w[:, g, :],
                                     vv[:, :, 64 * g:64 * g + 64], start=True, stop=True), "spatial", g)
            ada(1, 1)
            rows("even", "bz", tiles)
            evacuated(pe, "ada", 0, 5)
            for s in range(2):
                v = begin("gate", 0, s)
                for kt in range(KT):
                    mm = nc.tensor.matmul(v[:, P * kt:P * kt + P],
                                          mod[0][:, 2 * KT + kt, s:s + 1].broadcast_to([P, P]), ident[:],
                                          start=True, stop=True)
                end(mm, "gate", 0, s)
            for i, (what, dst) in enumerate((("q", qt), ("k", kt_))):
                ada(1, 2 + i)
                columns("even", "b" + what)
                for f in range(4):
                    evacuated(pe, "even", "b" + what, f)
                    v = begin("rope", what, f)
                    end(nc.tensor.matmul(v[:, 0:SEQ], rope_perm[:], dst[:, f, CTX:TOK], start=True, stop=True),
                        "rope", what, f)
            for g in range(8):
                evacuated(pe, "spatial", g)
            for kt in range(4):
                turn(("mix", "a", kt), [ao[:, m, P * kt:P * kt + P] for m in tiles], [P * m for m in tiles])
            for m in tiles:
                evacuated(pe, "even", "bv", m)
            pe.wait_ge(s_q, 4)
            pe.wait_ge(s_k, 4)

            def scores(u):
                m, h = u // 4, u % 4
                for i in range(2):
                    f = slice(64 * i, 64 * i + 64)
                    v = begin("S", "even", u, i)
                    for lo in range(0, keys(m), 512):
                        hi = min(lo + 512, keys(m))
                        mm = nc.tensor.matmul(v[:, lo:hi], qt[f, h, P * m:P * m + P], kt_[f, h, lo:hi], start=True,
                                              stop=True)
                    end(mm, "S", "even", u, i)

            scores(0)
            scores(1)
            for u in range(E_UNITS):
                m, h = u // 4, u % 4
                pe.wait_ge(s_comb, u + 1)
                turn(("T", "even", u), [p0[:, u % 3, P * n:P * n + P] for n in range(keys(m) // P)],
                     [P * n for n in range(keys(m) // P)])
                if u + 2 < E_UNITS:
                    scores(u + 2)
                v = begin("O", "even", u)
                evacuated(pe, "T", "even", u)
                last = keys(m) // P - 1
                for n in range(last + 1):
                    mm = nc.tensor.matmul(v[:, 0:P], pt[:, u % 2, P * n:P * n + P], vb[:, n, P * h:P * h + P],
                                          start=n == 0, stop=n == last)
                end(mm, "O", "even", u)
            pe.wait_ge(s_post, NT)
            for kt in range(4, 8):
                turn(("mix", "b", kt), [o_rows[:, m, P * (kt - 4):P * (kt - 4) + P] for m in tiles], [P * m for m in tiles])
            evacuated(pe, "mix", "b", 7)
            for c, what in enumerate("op"):
                rows("eout", what, tiles)
                ada(1, 4 + c)

            def xt_ready(*job):
                pe.wait_ge(s_xlo, plan.xt[job] + 1)

            def norm(stage, count):
                pe.wait_ge(s_xn2, count)
                for kt in range(KT):
                    turn(("norm", stage, kt), [h_rows[:, m, P * kt:P * kt + P] for m in range(NT)], norm_cols)

            lat = range(CT, NT)
            lat_cols = [P * m for m in range(LT)]
            norm("odd", NT)
            rows("odd", "a", tiles, made=1 * KT)
            ada(2, 0)
            rows("odd", "z", lat)
            pe.wait_ge(s_cn, NT)
            for kt in range(2):
                turn(("turn", "cq", kt), [a_rows[:, m, P * kt:P * kt + P] for m in lat], lat_cols)
            turn(("turn", "ckv", 0), [a_rows[:, m, 256:384] for m in tiles], [P * m for m in tiles])
            turn(("turn", "kr", 0), [a_rows[:, m, 384:512] for m in tiles], [P * m for m in tiles])
            evacuated(pe, "turn", "kr", 0)

            def permute(job, x):
                v = begin(*job)
                end(nc.tensor.matmul(v[:, 0:SEQ], rope_perm[:], x, start=True, stop=True), *job)

            permute(("rope", "kr", 0), kr_t[:, CTX:TOK])
            ada(2, 1)
            rows("odd", "y", lat)
            ada(2, 2)

            def attend(stage, units, score, keys_n, v_of, n):
                def s(u):
                    score(u, begin("S", stage, u))
                s(units[0])
                s(units[1])
                for i, u in enumerate(units):
                    evacuated(pe, "S", stage, u)
                    pbuf, pts = (po, ptb) if stage == "odd" else (pg, [ptg[:, 0, :], ptg[:, 1, :]])
                    turn(("T", stage, u), [pbuf[:, u % 3, P * a:P * a + P] for a in range(NT)], [P * a for a in range(NT)])
                    if i + 2 < len(units):
                        s(units[i + 2])
                    v = begin("O", stage, u)
                    evacuated(pe, "T", stage, u)
                    for a in range(NT):
                        mm = nc.tensor.matmul(v[:, 0:n], pts[u % 2][:, P * a:P * a + P], v_of(u, a), start=a == 0,
                                              stop=a == NT - 1)
                    end(mm, "O", stage, u)

            banks = ((0, 512), (512, TOK))

            def odd_scores(u, v):
                m, h = u % 16 // 4, u % 4
                half = slice(64 * (h % 2), 64 * (h % 2) + 64)
                for lo, hi in banks:
                    nc.tensor.matmul(v[:, lo:hi], q_n[:, h, P * m:P * m + P], k_n[:, h, lo:hi], start=True, stop=False)
                    mm = nc.tensor.matmul(v[:, lo:hi], q_r[half, h // 2, P * m:P * m + P], kr_t[half, lo:hi],
                                          start=False, stop=True)
                end(mm, "S", "odd", u)

            pe.wait_ge(s_ct_lo, 3)
            for g in range(2):
                k = splits[pieces[number[("q", g)]]["k"]]["k"]
                pe.wait_ge(s_lo, k + 1)
                wq = [x[:, k % SPLIT, 0:1536].rearrange("p (k n) -> p k n", k=2) for x in (whi, wlo)]
                for f in range(6):
                    v = begin("q", g, f)
                    for kt in range(2):
                        mm = three(v[:, 0:SEQ], [w[:, kt, P * f:P * f + P] for w in wq], (cqh[:, kt, :], cql[:, kt, :]),
                                   kt == 0, kt == 1)
                    end(mm, "q", g, f)
                k += 1
                pe.wait_ge(s_lo, k + 1)
                wkv = [x[:, k % SPLIT, 0:1024] for x in (whi, wlo)]
                for f in range(4):
                    v = begin("kv", g, f)
                    for lo, hi in banks:
                        mm = three(v[:, lo:hi], [w[:, P * f:P * f + P] for w in wkv], (ckvh[:, lo:hi], ckvl[:, lo:hi]),
                                   True, True)
                    end(mm, "kv", g, f)
                for m in tiles:
                    v = begin("v", g, m)
                    at_ = slice(P * m, P * m + P)
                    end(three(v[:, 0:512], (ckvh[:, at_], ckvl[:, at_]), [w[:, 512:1024] for w in wkv], True, True),
                        "v", g, m)
                for j in range(2):
                    evacuated(pe, "q", g, 4 + j)
                    permute(("rope", "qr", 2 * g + j), q_r[:, j, :])
                for f in range(4):
                    evacuated(pe, "kv", g, f)
                for m in tiles:
                    evacuated(pe, "v", g, m)
                pe.wait_ge(s_kr, 1)
                pe.wait_ge(s_qr, 2 * g + 2)
                attend("odd", range(16 * g, 16 * g + 16), odd_scores, NT,
                       lambda u, a: v_o[:, a, P * (u % 4):P * (u % 4) + P], P)
                ada(2, 3 + g)

            def gate(layer, first, n=0):
                v = begin("gate", layer, n)
                for kt in range(KT):
                    mm = nc.tensor.matmul(v[:, P * kt:P * kt + P],
                                          mod[layer][:, first + kt, 0:1].broadcast_to([P, P]), ident[:],
                                          start=True, stop=True)
                end(mm, "gate", layer, n)

            gate(1, 2 * KT)
            pe.wait_ge(s_oy, LT)
            for kt in range(KT):
                turn(("mix", "odd", kt), [oo_rows[:, m, P * kt:P * kt + P] for m in range(LT)], lat_cols)
            evacuated(pe, "mix", "odd", KT - 1)
            for c, what in enumerate("op"):
                rows("oout", what, lat)
                ada(2, 5 + c)

            norm("second", 2 * NT)
            rows("second", "qa", lat, made=2 * KT)
            ada(2, 7)
            rows("second", "kk", tiles)
            ada(2, 8)
            rows("second", "vr", tiles)
            ada(2, 9)
            rows("second", "gr", lat)
            ada(2, 10)
            rows("second", "qr", lat, 256)
            pe.wait_ge(s_qn, LT)
            for kt in range(4):
                turn(("turn", "qa", kt), [qa[:, m, P * kt:P * kt + P] for m in range(LT)], lat_cols)
            turn(("turn", "ka", 0), [kk[:, m, 0:P] for m in tiles], [P * m for m in tiles])
            for kt in range(2):
                turn(("turn", "qr2", kt), [qr[:, m, P * kt:P * kt + P] for m in range(LT)], lat_cols)
                turn(("turn", "kr2", kt), [kk[:, m, 256 + P * kt:384 + P * kt] for m in tiles], [P * m for m in tiles])
            ada(2, 11)
            gate(2, 2 * KT)
            for kt in range(4):
                evacuated(pe, "turn", "qa", kt)
            evacuated(pe, "turn", "ka", 0)
            for kt in range(2):
                evacuated(pe, "turn", "qr2", kt)
                evacuated(pe, "turn", "kr2", kt)

            def gqa_scores(u, v):
                m, h = u // 8, u % 8
                half = slice(64 * (h // 4), 64 * (h // 4) + 64)
                for lo, hi in banks:
                    mm = nc.tensor.matmul(v[:, lo:hi], qa_t[half, h % 4, P * m:P * m + P], ka_t[half, lo:hi], start=True,
                                          stop=True)
                end(mm, "S", "gqa", u)

            attend("gqa", range(S_UNITS), gqa_scores, NT,
                   lambda u, a: kk[:, a, P + 64 * (u % 8 // 4):P + 64 * (u % 8 // 4) + 64], 64)
            def decayed_scores(h, a):
                half = slice(64 * (h % 2), 64 * (h % 2) + 64)
                v = begin("R", h, a)
                end(nc.tensor.matmul(v[:, 0:SEQ], kr2_t[half, h // 2, P * a:P * a + P], qr_t[half, h // 2, :],
                                     start=True, stop=True), "R", h, a)

            for a in range(NT):
                decayed_scores(0, a)
            for h in range(R_HEADS):
                for b in range(NT):
                    if b == 2:
                        v = begin("RO", h)
                        for a in range(NT):
                            evacuated(pe, "R", h, a)
                        for m in range(LT):
                            for a in range(NT):
                                mm = nc.tensor.matmul(v[:, P * m:P * m + P], sw[:, a, P * m:P * m + P],
                                                      vr[:, a, P * h:P * h + P], start=a == 0, stop=a == NT - 1)
                        end(mm, "RO", h)
                    if h + 1 < R_HEADS:
                        decayed_scores(h + 1, b)
            pe.wait_ge(s_ret, R_HEADS)
            for kt in range(KT):
                source = oa_rows if kt < 4 else or_rows
                turn(("mix", "second", kt), [source[:, m, P * (kt % 4):P * (kt % 4) + P] for m in range(LT)], lat_cols)
            evacuated(pe, "mix", "second", KT - 1)
            for what in "op":
                rows("sout", what, lat)

            pe.wait_ge(s_mods, 1)
            v = begin("free", 0)
            mm = nc.tensor.matmul(v[:, 0:1], ident[:], ident[:, 0:1], start=True, stop=True)
            mm.then_inc(s_used, SPLIT)
            end(nc.tensor.matmul(v[:, 0:1], ident[:], ident[:, 0:1], start=True, stop=True), "free", 0)
            gate(2, 4 * KT, 1)
            gate(2, 3 * KT, 2)
            pe.wait_ge(s_row2, LT)
            for kt in range(KT):
                turn(("turn", "h2", kt), [h2[:, m, P * kt:P * kt + P] for m in range(LT)], lat_cols)
            evacuated(pe, "turn", "h2", KT - 1)
            v = begin("router")
            for m in range(LT):
                for kt in range(KT):
                    mm = nc.tensor.matmul(v[:, 36 * m:36 * m + 36], h2_t[:, kt, P * m:P * m + P], router_w[:, kt, :],
                                          start=kt == 0, stop=kt == KT - 1)
            end(mm, "router")
            pe.wait_ge(s_h2l, LT)
            v = begin("free", 1)
            mm = nc.tensor.matmul(v[:, 0:1], ident[:], ident[:, 0:1], start=True, stop=True)
            mm.then_inc(s_used, PARTS - SPLIT)
            end(nc.tensor.matmul(v[:, 0:1], ident[:], ident[:, 0:1], start=True, stop=True), "free", 1)
            v = begin("counts")
            pe.wait_ge(s_chosen, 1)
            both = tmp[:, 0, 544:672].rearrange("p (m n) -> p m n", m=LT)
            for m in range(LT):
                for a in range(m + 1):
                    nc.tensor.matmul(v[:, 32 * m:32 * m + 32], before if a == m else ones, both[:, a, :],
                                     start=a == 0, stop=a == m)
            for m in range(LT):
                mm = nc.tensor.matmul(v[0:EXPERTS, 512:513], both[:, m, :], ones[:, 0:1], start=m == 0, stop=m == LT - 1)
            end(mm, "counts")
            v = begin("starts")
            pe.wait_ge(s_nblk, 1)
            end(nc.tensor.matmul(v[:, 0:33], route[0:EXPERTS, 28:29].broadcast_to([EXPERTS, P]), before[0:EXPERTS, 0:33],
                                 start=True, stop=True), "starts")
            for job in (("turn", "h2", KT - 1), ("router",), ("counts",), ("starts",)):
                evacuated(pe, *job)

            pe.wait_ge(s_blocks, 1)
            last = pe.value_load(blocks_i[0:1, 40:41], min_val=7, max_val=BLOCKS - 1)

            def gather(j, h):
                pe.wait_ge(s_hot, j + 1)
                for m in range(LT):
                    for part in (h2h, h2l):
                        mm = nc.tensor.matmul(ps[:, h, :], hot[:, m, :], part[:, m, 512 * h:512 * h + 512],
                                              start=m == 0 and part is h2h, stop=m == LT - 1 and part is h2l)
                mm.then_inc(s_gat, 1)

            def turn_rows(j):
                for h in range(2):
                    pe.wait_ge(s_rows, 2 * j + h + 1)
                    for k in range(4):
                        mm = nc.tensor.transpose(ps[:, 2 + h, P * k:P * k + P],
                                                 xe_rows[:, 512 * h + P * k:512 * h + P * k + P], ident[:])
                    mm.then_inc(s_turned, 1)

            def in_product(j, i0, bank):
                for i in range(2):
                    pe.wait_ge(s_xeh, 2 * j + i + 1)
                    pe.wait_ge(s_xel, 2 * j + i + 1)
                    pe.wait_ge(s_el, PARTS * j + i0 + i + 1 + RAW)
                    for k in range(4):
                        w = tuple(x[i0 + i][:, WIDTH * k:WIDTH * k + WIDTH] for x in (weh, wel))
                        mm = three(ps[:, bank, :], (xeh[:, 4 * i + k, :], xel[:, 4 * i + k, :]), w,
                                   i + k == 0, i == 1 and k == 3)
                    mm.then_inc(s_used, 1)

            def block_of(j, nxt):
                pe.wait_ge(s_hth, j + 1)
                pe.wait_ge(s_htl, j + 1)
                in_product(j, 0, 4)
                in_product(j, 2, 5)
                if nxt:
                    gather(j + 1, 0)
                pe.wait_ge(s_hid, j + 1)
                for k in range(4):
                    mm = nc.tensor.transpose(ps[:, 4, P * k:P * k + P], hid[:, P * k:P * k + P], ident[:])
                mm.then_inc(s_tr, 1)
                if nxt:
                    gather(j + 1, 1)
                pe.wait_ge(s_hth, j + 2)
                pe.wait_ge(s_htl, j + 2)
                pe.wait_ge(s_yev, j + 1)
                for i in range(2):
                    pe.wait_ge(s_el, PARTS * j + 4 + i + 1 + RAW)
                    for k in range(2):
                        for n in range(2):
                            at_w = slice(D * k + 512 * n, D * k + 512 * n + 512)
                            mm = three(ps[:, 6 + n, :], (hth[:, 2 * i + k, :], htl[:, 2 * i + k, :]),
                                       (weh[4 + i][:, at_w], wel[4 + i][:, at_w]), i + k == 0, i + k == 2)
                    mm.then_inc(s_used, 1)
                    if nxt and i == 0:
                        turn_rows(j + 1)

            pe.wait_ge(s_h2h, LT)
            pe.wait_ge(s_h2l, LT)
            gather(0, 0)
            gather(0, 1)
            turn_rows(0)
            with pe.Fori(0, last) as j:
                block_of(j, True)
            block_of(last, False)
            pe.wait_ge(s_yev, last + 2)
            gate(2, 5 * KT, 3)



def rope_tables():
    row = np.repeat(np.arange(SEQ // 64), 64).astype(np.float32)
    col = np.tile(np.arange(64), SEQ // 64).astype(np.float32)
    inv = (np.float32(10000.0) ** (-np.arange(0, 32, 2, dtype=np.float32) / np.float32(32))).astype(np.float32)
    a, b = row[:, None] * inv[None], col[:, None] * inv[None]
    ang = np.concatenate([a, a, b, b], -1)
    cos, sin = np.cos(ang).astype(np.float32), np.sin(ang).astype(np.float32)
    perm = np.zeros((P, P), np.float32)
    for base in range(0, P, 32):
        for i in range(16):
            perm[base + 16 + i, base + i] = -1.0
            perm[base + i, base + 16 + i] = 1.0
    ang = np.repeat(np.concatenate([a, b], -1), 2, axis=-1)
    sign = np.tile(np.array([-1, 1], np.float32), 32)
    by_tile = lambda t: t.reshape(LT, P, 64).transpose(1, 0, 2).reshape(P, LT * 64).astype(np.float32)
    return (np.tile(cos.T, (2, 1)).copy(), np.tile(sin.T, (2, 1)).copy(), perm,
            by_tile(np.cos(ang)), by_tile(np.sin(ang).astype(np.float32) * sign))


def route_constants():
    c = np.zeros((P, 512), np.float32)
    c[:, 0:P] = np.arange(P)
    c[:, P:2 * P] = np.arange(P)[:, None] < np.arange(P)[None]
    c[:, 2 * P:3 * P] = 1
    c[:, 384:384 + BLOCKS + 1] = P * np.arange(BLOCKS + 1)
    c[:, 424:428] = P * np.arange(4)
    c[:, 428:460] = EXPERTS - np.arange(EXPERTS)
    return c


def kernel(**inputs):
    import numpy as _np
    import concourse.bacc as _bacc
    from concourse import mybir as _mybir
    from concourse.bass_utils import run_bass_kernel_spmd as _run

    a = {k: _np.asarray(v) for k, v in inputs.items()}

    def streamed(w):
        n = w.shape[1] // 512
        return w.reshape(2, 4, P, n, 512).transpose(3, 0, 2, 1, 4).reshape(n, 2, P, 2048)

    def on_partitions(v):
        return v.reshape(-1, P).T

    def everywhere(v):
        return _np.broadcast_to(v.reshape(1, -1), (P, v.size))

    cos_t, sin_t, perm, cos_r, sin_r = rope_tables()
    w = a["odd_w_in"][0]
    odd_in = _np.concatenate([w[:, 0:448], w[:, 384:448], w[:, 448:1472]], 1)
    w = a["c_wq_b"][0].reshape(2, P, 2, 4, 192)
    wq = _np.concatenate([w[..., 0:128].reshape(2, P, 2, 512), w[..., 128:192].reshape(2, P, 2, 256)], -1)
    wq = wq.transpose(2, 1, 0, 3).reshape(2, P, 1536)
    w = a["c_wkv_b"][0].reshape(P, 2, 4, 2, P)
    wkv = w.transpose(1, 0, 3, 2, 4).reshape(2, P, 1024)
    w = a["w_in_2"][0]
    second_in = _np.concatenate([
        w[:, 0:512].reshape(D, 2, 4, 64).transpose(0, 2, 1, 3).reshape(D, 512), w[:, 512:768], w[:, 1024:1280],
        w[:, 1280:1792], w[:, 1792:2304], w[:, 768:1024], w[:, 768:1024]], 1)
    x_all = _np.concatenate([a["ctx"][0], a["x"][0]], 0).reshape(NT, P, D)
    packed = {
        "x": x_all,
        "ident": _np.eye(P, dtype=_np.float32), "rope_perm": perm, "cos_t": cos_t, "sin_t": sin_t,
        "cvec": _np.stack([
            _np.stack([a["c"][0].reshape(KT, P).T, a["c_ctx"].reshape(KT, P).T], -1),
            _np.stack([a["c_2"][0].reshape(KT, P).T, a["c_ctx_2"].reshape(KT, P).T], -1)], 1),
        "vecs": _np.concatenate([
            on_partitions(a["norm_w"][0]), on_partitions(a["norm_w"][1]), on_partitions(a["norm1_g_2"][0]),
            on_partitions(a["ada_b"][0]), on_partitions(a["ada_b"][1]), on_partitions(a["b_ada_2"][0]),
            a["a_bs"][0].T, on_partitions(a["c_q_norm_w"][0]), on_partitions(a["c_kv_norm_w"][0]),
            everywhere(a["ret_decay_fwd_2"][0]), everywhere(a["ret_decay_bwd_2"][0])], 1),
        "spatial_w": a["a_ws"][0].transpose(2, 0, 1),
        "ln_w": everywhere(a["a_ln_w"][0]), "ln_b": everywhere(a["a_ln_b"][0]),
        "lamv": everywhere(_np.stack([a[f"b_{n}"][0] for n in ("lq1", "lk1", "lq2", "lk2")])).reshape(P, 4, 64),
        "subln": everywhere(a["b_subln_w"][0]),
        "ada0": streamed(a["ada_w"][0]), "ada1": streamed(a["ada_w"][1]), "ada2": streamed(a["w_ada_2"][0]),
        "even": streamed(a["even_w_in"][0]), "eout": streamed(a["even_w_out"][0]),
        "odd": streamed(odd_in), "q": wq, "kv": wkv, "oout": streamed(a["odd_w_out"][0]),
        "final_w": everywhere(a["final_w"]),
        "ctx2": a["ctx_2"][0].reshape(CT, P, D),
        "gn": everywhere(_np.stack([a["ret_gn_g_2"][0], a["ret_gn_b_2"][0]])).reshape(P, 2, 512),
        "cos_r": cos_r, "sin_r": sin_r,
        "qk_norm": everywhere(_np.stack([a["attn_q_norm_2"][0], a["attn_k_norm_2"][0]])),
        "route_c": route_constants(),
        "router": _np.concatenate([
            _np.concatenate([a["moe_w_grp_2"][0], a["moe_w_exp_2"][0]], 1).reshape(KT, P, 36).transpose(1, 0, 2)
            .reshape(P, KT * 36), everywhere(_np.concatenate([a["moe_b_grp_2"][0], a["moe_b_exp_2"][0]]))], 1),
        "norm2_g": on_partitions(a["norm2_g_2"][0]), "final_g": everywhere(a["final_norm_g_2"]),
        "experts": _np.concatenate(
            [a[f"moe_w_{n}_2"][0].reshape(EXPERTS, 2, 4, P, 512).transpose(0, 1, 3, 2, 4).reshape(EXPERTS, 2, P, 2048)
             for n in ("gate", "up")]
            + [a["moe_w_down_2"][0].reshape(EXPERTS, 2, 2, P, D).transpose(0, 1, 3, 2, 4).reshape(EXPERTS, 2, P, 2048)], 1),
        "second": streamed(second_in), "sout": streamed(a["w_out_2"][0]),
    }
    nc = _bacc.Bacc("TRN2", target_bir_lowering=False, num_devices=1)
    arrays, aps = {}, {}
    for name, v in packed.items():
        v = _np.ascontiguousarray(v)
        arrays[f"in_{name}"] = v
        aps[name] = nc.dram_tensor(f"in_{name}", v.shape, _mybir.dt.from_np(v.dtype), kind="ExternalInput").ap()
    out = nc.dram_tensor("out", (SEQ, D), F32, kind="ExternalOutput").ap()
    build(nc, aps, out)
    r = _run(nc, [arrays], core_ids=[0])
    return r.results[0]["out"].reshape(1, SEQ, D)
```
